# Optimizing a Trainium2 kernel written in Bass

```python
import math
import jax, jax.numpy as jnp
from jax import lax
import numpy as np

D_MODEL = 2048
BATCH = 1
SEQ = 1024
DEPTH = 1

CHUNK = 64
Q_BLOCK = 128
FOX_HEADS = 8
FOX_HEAD_DIM = 128
FOX_WIDTH = FOX_HEADS * FOX_HEAD_DIM
GDN_HEADS = 8
GDN_HEAD_DIM = 128
GDN_WIDTH = GDN_HEADS * GDN_HEAD_DIM
MIX_WIDTH = FOX_WIDTH + GDN_WIDTH
CONV_WIDTH = 4
EPS = 1e-6
IN_SIZES = (FOX_WIDTH, FOX_WIDTH, FOX_WIDTH, FOX_WIDTH, FOX_HEADS,
            GDN_WIDTH, GDN_WIDTH, GDN_WIDTH, GDN_WIDTH, GDN_HEADS, GDN_HEADS)
IN_WIDTH = 4 * FOX_WIDTH + FOX_HEADS + 4 * GDN_WIDTH + 2 * GDN_HEADS

kernel_name = "hybrid_fox_gdn_adaln_block"

def rmsnorm(x, g):
    xf = x.astype(jnp.float32)
    y = xf * lax.rsqrt(jnp.mean(xf * xf, axis=-1, keepdims=True) + EPS)
    return (y * g.astype(jnp.float32)).astype(x.dtype)

def l2norm(x):
    xf = x.astype(jnp.float32)
    return xf * lax.rsqrt(jnp.sum(xf * xf, axis=-1, keepdims=True) + EPS)

def to_heads(t, n_heads):
    b, s, w = t.shape
    return t.reshape(b, s, n_heads, w // n_heads).transpose(0, 2, 1, 3)

def from_heads(t):
    b, n, s, d = t.shape
    return t.transpose(0, 2, 1, 3).reshape(b, s, n * d)

def split_cols(p):
    idx = np.cumsum(np.array(IN_SIZES))[:-1].tolist()
    return jnp.split(p, idx, axis=-1)

def forgetting_attention(q, k, v, f_logit, b_f, qn_g, kn_g):
    b, s, _ = q.shape
    qh = rmsnorm(to_heads(q, FOX_HEADS), qn_g).astype(jnp.float32)
    kh = rmsnorm(to_heads(k, FOX_HEADS), kn_g).astype(jnp.float32)
    vh = to_heads(v, FOX_HEADS).astype(jnp.float32)
    log_f = jax.nn.log_sigmoid(f_logit.astype(jnp.float32) + b_f.astype(jnp.float32))
    F = jnp.cumsum(log_f, axis=1).transpose(0, 2, 1)
    nq = s // Q_BLOCK
    qb = qh.reshape(b, FOX_HEADS, nq, Q_BLOCK, FOX_HEAD_DIM).transpose(2, 0, 1, 3, 4)
    Fb = F.reshape(b, FOX_HEADS, nq, Q_BLOCK).transpose(2, 0, 1, 3)
    tb = jnp.arange(s, dtype=jnp.int32).reshape(nq, Q_BLOCK)
    s_pos = jnp.arange(s, dtype=jnp.int32)
    scale = FOX_HEAD_DIM ** -0.5

    def block(args):
        q_i, F_i, t_i = args
        logits = (jnp.einsum('bhqd,bhkd->bhqk', q_i, kh) * scale
                  + (F_i[..., :, None] - F[..., None, :]))
        mask = s_pos[None, :] <= t_i[:, None]
        logits = jnp.where(mask, logits, -jnp.inf)
        p = jax.nn.softmax(logits, axis=-1)
        return jnp.einsum('bhqk,bhkd->bhqd', p, vh)

    o = lax.map(block, (qb, Fb, tb))
    return o.transpose(1, 0, 3, 2, 4).reshape(b, s, FOX_WIDTH)

def causal_depthwise_conv(x, w):
    c = x.shape[-1]
    return lax.conv_general_dilated(
        x, w[:, None, :], window_strides=(1,), padding=[(CONV_WIDTH - 1, 0)],
        dimension_numbers=('NWC', 'WIO', 'NWC'), feature_group_count=c)

def chunk_gated_delta_rule(q, k, v, g, beta):
    b, h, s, dk = q.shape
    dv = v.shape[-1]
    n = s // CHUNK
    q = q.reshape(b, h, n, CHUNK, dk)
    k = k.reshape(b, h, n, CHUNK, dk)
    v = v.reshape(b, h, n, CHUNK, dv)
    g = g.reshape(b, h, n, CHUNK)
    beta = beta.reshape(b, h, n, CHUNK)
    gc = jnp.cumsum(g, axis=-1)
    idx = jnp.arange(CHUNK)
    lower = idx[:, None] >= idx[None, :]
    strict = idx[:, None] > idx[None, :]
    decay = jnp.exp(jnp.where(lower, gc[..., :, None] - gc[..., None, :], -jnp.inf))
    kb = k * beta[..., None]
    vb = v * beta[..., None]
    M = jnp.where(strict, jnp.einsum('bhncd,bhnsd->bhncs', kb, k) * decay, 0.0)
    A = M + jnp.eye(CHUNK, dtype=jnp.float32)
    rhs = jnp.concatenate([vb, kb * jnp.exp(gc)[..., None]], axis=-1)
    sol = lax.linalg.triangular_solve(A, rhs, left_side=True, lower=True, unit_diagonal=True)
    u, w = sol[..., :dv], sol[..., dv:]
    attn = jnp.where(lower, jnp.einsum('bhncd,bhnsd->bhncs', q, k) * decay, 0.0)

    def step(state, xs):
        q_i, k_i, u_i, w_i, gc_i, attn_i = xs
        v_new = u_i - jnp.einsum('bhcd,bhde->bhce', w_i, state)
        o_i = (jnp.einsum('bhcd,bhde->bhce', q_i * jnp.exp(gc_i)[..., None], state)
               + jnp.einsum('bhcs,bhse->bhce', attn_i, v_new))
        g_last = gc_i[..., -1]
        k_dec = k_i * jnp.exp(g_last[..., None] - gc_i)[..., None]
        new_state = state * jnp.exp(g_last)[..., None, None] + jnp.einsum('bhcd,bhce->bhde', k_dec, v_new)
        return new_state, o_i

    mv = lambda t: jnp.moveaxis(t, 2, 0)
    state0 = jnp.zeros((b, h, dk, dv), jnp.float32)
    _, o = lax.scan(step, state0, (mv(q), mv(k), mv(u), mv(w), mv(gc), mv(attn)))
    return o.transpose(1, 2, 0, 3, 4).reshape(b, h, s, dv)

def gated_deltanet(q, k, v, a, bt, conv_w, A_log, dt_bias, norm_g):
    qkv = jnp.concatenate([q, k, v], axis=-1).astype(jnp.float32)
    qkv = jax.nn.silu(causal_depthwise_conv(qkv, conv_w.astype(jnp.float32)))
    q, k, v = jnp.split(qkv, 3, axis=-1)
    qh = l2norm(to_heads(q, GDN_HEADS)) * (GDN_HEAD_DIM ** -0.5)
    kh = l2norm(to_heads(k, GDN_HEADS))
    vh = to_heads(v, GDN_HEADS)
    beta = jax.nn.sigmoid(bt.astype(jnp.float32)).transpose(0, 2, 1)
    g = (-jnp.exp(A_log.astype(jnp.float32))
         * jax.nn.softplus(a.astype(jnp.float32) + dt_bias.astype(jnp.float32))).transpose(0, 2, 1)
    o = chunk_gated_delta_rule(qh, kh, vh, g, beta)
    o = rmsnorm(o, norm_g)
    return from_heads(o)

def setup_inputs(seed: int = 0) -> dict:
    key = jax.random.key(seed)
    ks = jax.random.split(key, 16)
    f32 = jnp.float32
    x = jax.random.normal(ks[0], (BATCH, SEQ, D_MODEL), f32)
    c = jax.random.normal(ks[1], (BATCH, D_MODEL), f32)
    norm_g = 1.0 + 0.02 * jax.random.normal(ks[2], (DEPTH, D_MODEL), f32)
    w_ada = 0.5 * D_MODEL ** -0.5 * jax.random.normal(ks[3], (DEPTH, D_MODEL, 3 * D_MODEL), f32)
    b_ada = 0.01 * jax.random.normal(ks[4], (DEPTH, 3 * D_MODEL), f32)
    w_in = D_MODEL ** -0.5 * jax.random.normal(ks[5], (DEPTH, D_MODEL, IN_WIDTH), f32)
    b_fgate = jax.random.uniform(ks[6], (DEPTH, FOX_HEADS), f32, 1.0, 4.0)
    fox_qn_g = 1.0 + 0.02 * jax.random.normal(ks[7], (DEPTH, FOX_HEAD_DIM), f32)
    fox_kn_g = 1.0 + 0.02 * jax.random.normal(ks[8], (DEPTH, FOX_HEAD_DIM), f32)
    gdn_conv_w = CONV_WIDTH ** -0.5 * jax.random.normal(ks[9], (DEPTH, CONV_WIDTH, 3 * GDN_WIDTH), f32)
    gdn_A_log = jnp.log(jax.random.uniform(ks[10], (DEPTH, GDN_HEADS), f32, 1.0, 16.0))
    dt = jnp.exp(jax.random.uniform(ks[11], (DEPTH, GDN_HEADS), f32, math.log(1e-3), math.log(1e-1)))
    gdn_dt_bias = dt + jnp.log(-jnp.expm1(-dt))
    gdn_norm_g = 1.0 + 0.02 * jax.random.normal(ks[12], (DEPTH, GDN_HEAD_DIM), f32)
    w_out = MIX_WIDTH ** -0.5 * jax.random.normal(ks[13], (DEPTH, MIX_WIDTH, D_MODEL), f32)
    final_g = 1.0 + 0.02 * jax.random.normal(ks[14], (D_MODEL,), f32)
    return {"x": x, "c": c, "norm_g": norm_g, "w_ada": w_ada, "b_ada": b_ada,
            "w_in": w_in, "b_fgate": b_fgate, "fox_qn_g": fox_qn_g, "fox_kn_g": fox_kn_g,
            "gdn_conv_w": gdn_conv_w, "gdn_A_log": gdn_A_log, "gdn_dt_bias": gdn_dt_bias,
            "gdn_norm_g": gdn_norm_g, "w_out": w_out, "final_g": final_g}

def reference(x, c, norm_g, w_ada, b_ada, w_in, b_fgate, fox_qn_g, fox_kn_g,
              gdn_conv_w, gdn_A_log, gdn_dt_bias, gdn_norm_g, w_out, final_g):
    c_act = jax.nn.silu(c)
    for l in range(DEPTH):
        mod = c_act @ w_ada[l] + b_ada[l]
        shift, scale, gate = jnp.split(mod, 3, axis=-1)
        h = rmsnorm(x, norm_g[l]) * (1.0 + scale[:, None, :]) + shift[:, None, :]
        p = h @ w_in[l]
        fq, fk, fv, fz, ff, gq, gk, gv, gz, ga, gb = split_cols(p)
        fox_o = forgetting_attention(fq, fk, fv, ff, b_fgate[l], fox_qn_g[l], fox_kn_g[l])
        fox_o = fox_o * jax.nn.silu(fz.astype(jnp.float32))
        gdn_o = gated_deltanet(gq, gk, gv, ga, gb, gdn_conv_w[l], gdn_A_log[l],
                               gdn_dt_bias[l], gdn_norm_g[l])
        gdn_o = gdn_o * jax.nn.silu(gz.astype(jnp.float32))
        mixed = jnp.concatenate([fox_o, gdn_o], axis=-1).astype(x.dtype)
        x = x + gate[:, None, :] * (mixed @ w_out[l])
    return rmsnorm(x, final_g)


_drawn_inputs = setup_inputs


def setup_inputs(seed=0):
    import zlib

    import numpy as np

    out = dict(_drawn_inputs(seed))
    spreads = {}
    factors = {'norm_g': 8.0,
     'b_ada': 8.0,
     'fox_qn_g': 8.0,
     'fox_kn_g': 8.0,
     'gdn_A_log': 3.816,
     'gdn_norm_g': 8.0,
     'final_g': 2.781}
    for name, (base, spread) in spreads.items():
        noise = np.random.default_rng([zlib.crc32(name.encode()), seed]).standard_normal(out[name].shape)
        drawn = base * np.exp(spread * noise) if base else spread * noise
        out[name] = __import__('jax').numpy.asarray(drawn.astype(out[name].dtype))
    for name, factor in factors.items():
        out[name] = (out[name] * factor).astype(out[name].dtype)
    return out
```

```python
from contextlib import ExitStack

import numpy as np
import concourse.bass as bass
from concourse import mybir

ALU = mybir.AluOpType
ACT = mybir.ActivationFunctionType
F32 = mybir.dt.float32
F32R = mybir.dt.float32r
BF16 = mybir.dt.bfloat16

P = 128
BIG = 3.0e38
EPS = 1e-6


def hybrid_block(nc, x, c, norm_g, w_ada, b_ada, w_in, b_fgate, fox_qn_g, fox_kn_g,
                 gdn_conv_w, gdn_A_log, gdn_dt_bias, gdn_norm_g, w_out, final_g, out):
    SEQ, D = x.shape[1], x.shape[2]
    H = b_fgate.shape[1]
    HD = fox_qn_g.shape[1]
    TAPS = gdn_conv_w.shape[1]
    KT = D // P
    NB = SEQ // P
    HALF = 512
    assert SEQ == 2 * HALF and HD == P and H == 8 and KT == 16 and TAPS == 4
    FW = H * HD
    SCALE = float(HD) ** -0.5
    SLOTS = 4 * KT
    COL_F = FW * 4
    COL_G = FW * 4 + H
    COL_AB = COL_G + 4 * FW
    FOX_COL = (0, FW, 3 * FW, 2 * FW)
    GDN_COL = (COL_G + 2 * FW, COL_G, COL_G + FW, COL_G + 3 * FW)
    CONV_AT = (2, 0, 1)
    LEVELS = 7

    xs = x[0]
    outs = out[0]
    w_in_v = w_in[0].rearrange("(t p) n -> p t n", p=P)
    w_out_v = w_out[0].rearrange("(t p) n -> p t n", p=P)
    w_ada_v = w_ada[0].rearrange("(t p) n -> p t n", p=P)

    rows_dram = nc.dram_tensor("rows_scratch", (2, H, SEQ), F32, kind="Internal").ap()
    mixed_dram = nc.dram_tensor("mixed_scratch", (2 * H, P, SEQ), F32, kind="Internal").ap()
    gate_dram = nc.dram_tensor("gate_scratch", (1, D), F32, kind="Internal").ap()

    with ExitStack() as ctx:
        def sb(name, shape, dt=F32, stack=ctx):
            return stack.enter_context(nc.sbuf_tensor(name, shape, dt))

        def sem(name):
            return ctx.enter_context(nc.semaphore(name))

        ps = ctx.enter_context(nc.psum_tensor("ps", [P, 8, HALF], F32))

        def flat(ap):
            return ap.rearrange("p a b -> p (a b)")

        pair = [flat(ps[:, 0:2, :]), flat(ps[:, 2:4, :])]
        mAB = flat(ps[:, 4:6, :])
        mA, mB, mC, mD = (ps[:, i, :] for i in (4, 5, 6, 7))

        eps = sb("eps", [P, 1])
        dummy = sb("dve_dummy", [P, 1])
        xstat = sb("xstat", [P, 32])
        cols = sb("cols", [P, 5 * KT + 3])
        c_col, g_col, b_col = cols[:, 0:KT], cols[:, KT:2 * KT], cols[:, 2 * KT:5 * KT]
        qgain, kgain, ngain = (cols[:, 5 * KT + i:5 * KT + i + 1] for i in range(3))
        a_col = sb("a_col", [P, KT])
        s_col = sb("s_col", [P, KT])
        mod = sb("mod", [P, 2 * KT])
        gatecol = sb("gatecol", [P, 4])
        hconv = sb("hconv", [P, 3, TAPS])
        hcol = sb("hcol", [P, 2 * NB])
        negbeta = sb("negbeta", [P, NB])
        negbg = sb("negbg", [P, NB])
        edl = sb("edl", [P, NB])
        eg = sb("eg", [P, NB])
        negmax = sb("negmax", [P, NB])
        lsum = sb("lsum", [P, NB])
        rsum = sb("rsum", [P, NB])
        ident = sb("ident", [P, P])
        ones = sb("ones", [P, P])
        causal_fox = sb("causal_fox", [P, P])
        causal_t = sb("causal_t", [P, P])
        strict = sb("strict", [P, P])
        level = sb("level", [P, LEVELS, P], BF16)
        gcol = sb("gcol", [P, H, 2 * NB])
        convw = sb("convw", [P, TAPS * 3 * H])

        begin = ExitStack()
        x_in = sb("x_in", [P, 4, D], F32, begin)
        ada = sb("ada", [P, 6, D], F32, begin)
        acc = sb("acc", [P, 2, D], F32, begin)
        junk = sb("junk", [P, D], F32, begin)
        rows_in = sb("rows_in", [P, 2, P], F32, begin)
        sb("begin_pad", [P, 2 * KT * SEQ - 13 * D - 2 * P], F32, begin)
        xT = sb("xT", [P, KT, SEQ], F32, begin)
        begin.close()

        main = ExitStack()
        h_hi = sb("h_hi", [P, KT, SEQ], F32R, main)
        h_lo = sb("h_lo", [P, KT, SEQ], F32R, main)
        fq = sb("fq", [P, SEQ], F32, main)
        fk = sb("fk", [P, SEQ], F32, main)
        fv = sb("fv", [P, NB, P], F32, main)
        fz = sb("fz", [P, SEQ], F32, main)
        gq = sb("gq", [P, SEQ], F32, main)
        gk = sb("gk", [P, SEQ], F32, main)
        gv = sb("gv", [P, NB, P], F32, main)
        gz = sb("gz", [P, SEQ], F32, main)
        vT = sb("vT", [P, SEQ], F32, main)
        scr = sb("scr", [P, 6 * SEQ], F32, main)
        small = sb("small", [P, 6, P], F32, main)
        sb("main_pad", [P, KT * SEQ - 15 * SEQ - 6 * P], F32, main)
        wr_hi = sb("wr_hi", [P, 4, 4, P], F32R, main)
        wr_lo = sb("wr_lo", [P, 4, 4, P], F32R, main)
        w_raw = sb("w_raw", [P, 4, 4, P], F32, main)
        main.close()

        tail = ExitStack()
        m_hi = sb("m_hi", [P, KT, SEQ], F32R, tail)
        m_lo = sb("m_lo", [P, KT, SEQ], F32R, tail)
        y = sb("y", [P, 4, D], F32, tail)
        gate_all = sb("gate_all", [P, D], F32, tail)
        fg_all = sb("fg_all", [P, D], F32, tail)
        gated = sb("gated", [P, 4, HALF], F32, tail)
        sq_out = sb("sq_out", [P, 2, HALF], F32, tail)
        sb("tail_pad", [P, KT * SEQ - 6 * D - 6 * HALF], F32, tail)
        wo_hi = sb("wo_hi", [P, 4, HALF], F32R, tail)
        wo_lo = sb("wo_lo", [P, 4, HALF], F32R, tail)
        wo_raw = sb("wo_raw", [P, 4, HALF], F32, tail)
        tail.close()

        def view(i, n=1):
            return scr[:, i * SEQ:(i + n) * SEQ]

        f_bias, f_s, f_pt = view(0), [view(1), view(2)], view(3).rearrange("p (b q) -> p b q", q=P)
        g_dec = view(0)
        g_kdec = view(1)
        g_att = view(2)
        g_u = view(3)
        g_nt, g_o = view(4), view(4)
        g_t = view(5)
        g_n = vT[:, :]
        state = [small[:, 0, :], small[:, 1, :]]
        ybuf = [small[:, 2, :], small[:, 3, :]]
        vnew = [small[:, 4, :], small[:, 5, :]]
        acc_gate = scr[:, 0:D]
        ada_gate = [scr[:, D:2 * D], scr[:, 2 * D:3 * D]]

        consts = sem("consts")
        gates_zeroed = sem("gates_zeroed")
        gates_w_put = sem("gates_w_put")
        cols_turned = sem("cols_turned")
        cols_ready = sem("cols_ready")
        consts_done = sem("consts_done")
        small_in = sem("small_in")
        gates_w_in = sem("gates_w_in")
        silu_c = sem("silu_c")
        x_sq = sem("x_sq")
        x_ln = sem("x_ln")
        x_rstd = sem("x_rstd")
        x_scaled = sem("x_scaled")
        x_turned = sem("x_turned")
        x_kept = sem("x_kept")
        ada_added = sem("ada_added")
        mod_summed = sem("mod_summed")
        mod_biased = sem("mod_biased")
        mod_cols = sem("mod_cols")
        h_affine = sem("h_affine")
        h_hi_done = sem("h_hi_done")
        h_lo_even = sem("h_lo_even")
        h_lo_odd = sem("h_lo_odd")
        w_zeroed = sem("w_zeroed")
        w_hi = sem("w_hi")
        w_lo = sem("w_lo")
        w_used = sem("w_used")
        gates_dve = sem("gates_dve")
        gates_act = sem("gates_act")
        gates_turned = sem("gates_turned")
        gates_cols = sem("gates_cols")
        rows_stored = sem("rows_stored")
        gate_biased = sem("gate_biased")
        gate_added = sem("gate_added")
        gate_summed = sem("gate_summed")
        gate_row = sem("gate_row")
        gate_stored = sem("gate_stored")
        fox_taken = sem("fox_taken")
        fox_sq = sem("fox_sq")
        fox_ss = sem("fox_ss")
        fox_ln = sem("fox_ln")
        fox_rstd = sem("fox_rstd")
        fox_qk = sem("fox_qk")
        fox_vturn = sem("fox_vturn")
        fox_v = sem("fox_v")
        fox_bias_in = sem("fox_bias_in")
        fox_masked = sem("fox_masked")
        fox_scores = sem("fox_scores")
        fox_max = sem("fox_max")
        fox_exp = sem("fox_exp")
        fox_recip = sem("fox_recip")
        fox_probs = sem("fox_probs")
        fox_pturn = sem("fox_pturn")
        fox_pt = sem("fox_pt")
        fox_pv = sem("fox_pv")
        fox_half = sem("fox_half")
        mixed_stored = sem("mixed_stored")
        head_conv = sem("head_conv")
        conv_first = sem("conv_first")
        conv_tap = sem("conv_tap")
        conv_silu = sem("conv_silu")
        dec_in = sem("dec_in")
        gdn_z = sem("gdn_z")
        gdn_cols = sem("gdn_cols")
        gdn_cexp = sem("gdn_cexp")
        gdn_sq = sem("gdn_sq")
        gdn_ss = sem("gdn_ss")
        gdn_ln = sem("gdn_ln")
        gdn_rstd = sem("gdn_rstd")
        gdn_qk = sem("gdn_qk")
        gdn_vturn = sem("gdn_vturn")
        gdn_v = sem("gdn_v")
        gdn_kturn = sem("gdn_kturn")
        gdn_kdec = sem("gdn_kdec")
        gdn_args = sem("gdn_args")
        gdn_decays = sem("gdn_decays")
        gdn_gram = sem("gdn_gram")
        gdn_att_mm = sem("gdn_att_mm")
        gdn_n = sem("gdn_n")
        gdn_att = sem("gdn_att")
        gdn_qe = sem("gdn_qe")
        gdn_nturn = sem("gdn_nturn")
        gdn_nt = sem("gdn_nt")
        gdn_t1 = sem("gdn_t1")
        gdn_uturn = sem("gdn_uturn")
        gdn_u1 = sem("gdn_u1")
        inv_p = sem("inv_p")
        inv_p_out = sem("inv_p_out")
        inv_t = sem("inv_t")
        inv_t_out = sem("inv_t_out")
        inv_u = sem("inv_u")
        inv_u_out = sem("inv_u_out")
        scan_z = sem("scan_z")
        scan_y = sem("scan_y")
        scan_v = sem("scan_v")
        scan_vnew = sem("scan_vnew")
        scan_upd = sem("scan_upd")
        scan_state = sem("scan_state")
        scan_o = sem("scan_o")
        scan_o_out = sem("scan_o_out")
        out_sq = sem("out_sq")
        out_ss = sem("out_ss")
        out_ln = sem("out_ln")
        out_rstd = sem("out_rstd")
        out_norm = sem("out_norm")
        gdn_done = sem("gdn_done")
        wo_hi_done = sem("wo_hi_done")
        wo_lo_done = sem("wo_lo_done")
        wo_used = sem("wo_used")
        tail_rows_in = sem("tail_rows_in")
        m_hi_done = sem("m_hi_done")
        m_lo_done = sem("m_lo_done")
        x_again = sem("x_again")
        y_ready = sem("y_ready")
        y_gated = sem("y_gated")
        y_added = sem("y_added")
        y_sq = sem("y_sq")
        y_sum = sem("y_sum")
        y_ln = sem("y_ln")
        y_rstd = sem("y_rstd")
        y_done = sem("y_done")
        y_stored = sem("y_stored")
        x_loaded = [sem(f"x_loaded{i}") for i in range(4)]
        ada_loaded = [sem(f"ada_loaded{i}") for i in range(6)]
        w_loaded = [sem(f"w_loaded{i}") for i in range(4)]
        gate_loaded = [sem("gate_loaded0"), sem("gate_loaded1")]
        m_loaded = [sem("m_loaded0"), sem("m_loaded1")]
        wo_loaded = [sem(f"wo_loaded{i}") for i in range(4)]

        def blocks(ap, n=NB):
            return ap.rearrange("p (b q) -> p b q", b=n)

        def blk(ap, j):
            return ap[:, j * P:(j + 1) * P]

        def half(ap, g):
            return ap[:, g * HALF:(g + 1) * HALF]

        def spread(col, n):
            return col.unsqueeze(2).to_broadcast([P, n, P])

        def over_blocks(mat, n):
            return mat.unsqueeze(1).to_broadcast([P, n, P])

        def flatb(t):
            return t[:, :, :].rearrange("p b q -> p (b q)")

        GATES_ROWS = 2 + 8 + 1 + NB + 2

        def scale_x(dve, t):
            dve.wait_ge(x_rstd, t + 1)
            dve.tensor_scalar(x_in[:, t % 4, :], x_in[:, t % 4, :], xstat[:, 16 + t:17 + t], None, ALU.mult)\
                .then_inc(x_scaled, 1)

        def keep(act, t):
            for g in range(4):
                act.wait_ge(x_turned, 4 * t + g + 1)
                act.activation(xT[:, 4 * g:4 * g + 4, t * P:(t + 1) * P],
                               (mA, mB, mC, mD)[g].rearrange("p (i q) -> p i q", q=P), ACT.Copy)\
                    .then_inc(x_kept, 1)

        def is_zero(m):
            return isinstance(m, int) and m == 0

        B0, A0 = 5, 9

        def n_groups(n):
            return 2 if NB - n > 4 else 1

        def groups_before(n):
            return 2 * n if n < 4 else 8 + (n - 4)

        GROUPS = groups_before(NB)

        def fox_slot(n):
            return 7 + 7 * n

        INV0 = 14
        SCAN0 = INV0 + 2 * (LEVELS - 1) + 1

        def scan_slot(j):
            return SCAN0 + 4 * j

        def add_x(pool, idx, t):
            hf, ch = idx // 4, idx % 4
            pool.wait_ge(y_gated, 4 * idx + t + 1)
            if ch == 0:
                pool.wait_ge(x_again, 64 * hf + 64)
            dst = y[:, t, ch * HALF:(ch + 1) * HALF]
            pool.tensor_tensor(dst, dst, gated[:, t, :], ALU.add).then_inc(y_added, 1)

        block = ctx.enter_context(nc.Block())

        @block.sync
        def _(sp):
            def load_x(t):
                if t >= 4:
                    sp.wait_ge(x_turned, 4 * (t - 3))
                sp.dma_start(x_in[:, t % 4, :], xs[t * P:(t + 1) * P, :]).then_inc(x_loaded[t % 4], 16)

            def load_ada(n):
                kt, part = n // 2, n % 2
                if n >= 6:
                    sp.wait_ge(ada_added, n - 5)
                sp.dma_start(ada[:, n % 6, :], w_ada_v[:, kt, part * D:(part + 1) * D])\
                    .then_inc(ada_loaded[n % 6], 16)

            load_x(0)
            for n in range(2 * KT):
                load_ada(n)
                if n % 3 == 0 and n // 3 + 1 < NB:
                    load_x(n // 3 + 1)

            def load_w(b, p, src, col):
                sp.wait_ge(w_lo, 4 * b + p - 3)
                sp.dma_start(w_raw[:, p, :, :], src[:, 4 * p:4 * p + 4, col]).then_inc(w_loaded[p], 16)

            for n in range(4):
                for p in range(4):
                    load_w(1 + n, p, w_in_v, slice(FOX_COL[n], FOX_COL[n] + P))
                    if n >= 2:
                        for kt in range(2 * (4 * n + p) - KT, 2 * (4 * n + p) - KT + 2):
                            if kt >= 2:
                                sp.wait_ge(gate_added, kt - 1)
                            sp.dma_start(ada_gate[kt % 2], w_ada_v[:, kt, 2 * D:3 * D])\
                                .then_inc(gate_loaded[kt % 2], 16)
                    if n == 2 and p == 3:
                        sp.wait_ge(gates_dve, GATES_ROWS)
                        sp.dma_start(rows_dram[0], gq[0:H, :]).then_inc(rows_stored, 16)
                        sp.dma_start(rows_dram[1], gq[32:32 + H, :]).then_inc(rows_stored, 16)
            sp.wait_ge(gate_added, KT)
            sp.dma_start(ada_gate[0][0:1, :], b_ada[:, 2 * D:3 * D]).then_inc(gate_biased, 16)
            sp.wait_ge(gate_row, 1)
            sp.dma_start(gate_dram, ada_gate[1][0:1, :]).then_inc(gate_stored, 16)

            def part_B(m, col):
                for n in range(4):
                    for p in range(4):
                        load_w(8 * m + B0 + n, p, w_in_v, bass.ds(col + GDN_COL[n], P))
                    if n == 0:
                        if not is_zero(m):
                            sp.wait_ge(gdn_done, m)
                        sp.dma_start(f_bias, rows_dram[0, bass.ds(m, 1), :].to_broadcast([P, SEQ]))\
                            .then_inc(fox_bias_in, 16)
                        store_gdn(m)

            def store_gdn(m):
                if not is_zero(m):
                    sp.dma_start(mixed_dram[bass.ds(m + H - 1, 1)].rearrange("o p t -> (o p) t"), g_o)\
                        .then_inc(mixed_stored, 16)

            def part_A(m, col):
                for n in range(4):
                    for p in range(4):
                        load_w(8 * m + A0 + n, p, w_in_v, bass.ds(col + FOX_COL[n] + P, P))
                    if n == 0:
                        head_in(m)

            def head_in(m):
                sp.wait_ge(fox_half, 2 * m + 2)
                sp.dma_start(g_dec, rows_dram[1, bass.ds(m, 1), :].to_broadcast([P, SEQ]))\
                    .then_inc(dec_in, 16)
                sp.dma_start(mixed_dram[bass.ds(m, 1)].rearrange("o p t -> (o p) t"), fz[:, :])\
                    .then_inc(mixed_stored, 16)

            sp.wait_ge(rows_stored, 32)
            sp.wait_ge(gate_stored, 16)
            part_B(0, 0)
            part_A(0, 0)
            with sp.Fori(1, H - 1) as m:
                col = sp.snap(m * P)
                part_B(m, col)
                part_A(m, col)
            part_B(H - 1, (H - 1) * P)
            head_in(H - 1)

            def load_wo(q, m, col):
                sp.wait_ge(wo_lo_done, q - 3)
                sp.dma_start(wo_raw[:, m % 4, :], w_out_v[:, m, col]).then_inc(wo_loaded[m % 4], 16)

            sp.wait_ge(w_used, 4 * (8 * H + 1))
            for m in range(4):
                sp.dma_start(wo_raw[:, m, :], w_out_v[:, m, 0:HALF]).then_inc(wo_loaded[m], 16)
            order = [i for i in range(2 * H - 1) if i != H - 1]
            sp.wait_ge(mixed_stored, 16 * 2 * H - 16)
            for n, i in enumerate(order):
                if n >= 2:
                    sp.wait_ge(m_lo_done, n - 1)
                sp.dma_start([fq, fk][n % 2][:, :], mixed_dram[i]).then_inc(m_loaded[n % 2], 16)

            def load_x_again(hf, t):
                if hf:
                    sp.wait_ge(y_stored, 16 * 4)
                sp.dma_start(y[:, t, :], xs[(4 * hf + t) * P:(4 * hf + t + 1) * P, :]).then_inc(x_again, 16)

            sp.wait_ge(m_lo_done, 2 * H)
            for t in range(4):
                load_x_again(0, t)
            sp.dma_start(gate_all[:, :], gate_dram.to_broadcast([P, D])).then_inc(tail_rows_in, 16)
            sp.dma_start(fg_all[:, :], final_g.rearrange("(a n) -> a n", a=1).to_broadcast([P, D]))\
                .then_inc(tail_rows_in, 16)
            def store_y(hf, t):
                sp.wait_ge(y_done, 4 * hf + t + 1)
                sp.dma_start(outs[(4 * hf + t) * P:(4 * hf + t + 1) * P, :], y[:, t, :]).then_inc(y_stored, 16)

            for idx in range(8):
                for m in range(KT):
                    q = idx * KT + m
                    if q >= 4:
                        load_wo(q, m, slice(idx % 4 * HALF, (idx % 4 + 1) * HALF))
                    if idx == 4 and m in (5, 7, 9, 11):
                        store_y(0, (m - 5) // 2)
                    if idx == 4 and m >= 12:
                        load_x_again(1, m - 12)
            for t in range(4):
                store_y(1, t)
            sp.wait_ge(y_stored, 16 * NB)

        @block.gpsimd
        def _(pool):
            pool.memset(w_raw[:, :, :, :], 0.0).then_inc(w_zeroed, 1)
            pool.memset(gatecol[:, :], 0.0).then_inc(gates_zeroed, 1)
            pool.wait_ge(gates_zeroed, 1)
            pool.memset(gatecol[0:32, 0:1], -1.0).then_inc(gates_zeroed, 1)
            pool.wait_ge(gates_zeroed, 2)
            pool.memset(gatecol[32:64, 0:1], 1.0).then_inc(gates_zeroed, 1)
            pool.wait_ge(gates_zeroed, 3)
            n = 0
            for t, v in ((ident, 0.0), (ones, 1.0), (causal_fox, 0.0), (causal_t, 0.0), (strict, 0.0),
                         (level, 1.0)):
                pool.memset(t[tuple([slice(None)] * len(t.shape))], v).then_inc(consts, 1)
                n += 1
            pool.memset(eps[:, :], EPS).then_inc(consts, 1)
            n += 1
            pool.wait_ge(consts, n)
            for t, op, fill, step in ((ident, ALU.not_equal, 1.0, (-1, 1)), (causal_fox, ALU.is_ge, -BIG, (-1, 1)),
                                      (causal_t, ALU.is_ge, -BIG, (1, -1)), (strict, ALU.is_gt, BIG, (-1, 1))):
                pool.affine_select(out=t[:, :], in_=t[:, :], compare_op=op, fill=fill, base=0,
                                   pattern=[[step[0], P]], channel_multiplier=step[1]).then_inc(consts, 1)
                n += 1
            for lv in range(LEVELS):
                size = 1 << lv
                cols = P // (2 * size)
                v = level[:, lv, :].rearrange("p (b u s) -> p b u s", u=2, s=size)
                for base, pat, cm in ((-size, [[-2 * size, cols], [0, 2], [0, size]], 1),
                                      (2 * size - 1, [[2 * size, cols], [0, 2], [0, size]], -1),
                                      (0, [[0, cols], [-1, 2], [0, size]], 0)):
                    pool.wait_ge(consts, n)
                    pool.affine_select(out=v, in_=v, compare_op=ALU.is_ge, fill=0.0, base=base,
                                       pattern=pat, channel_multiplier=cm).then_inc(consts, 1)
                    n += 1
            pool.wait_ge(gates_w_in, 32)
            pool.tensor_copy(w_raw[:, :, :, 64:64 + H], w_raw[:, :, :, 32 + H:32 + 2 * H]).then_inc(gates_w_put, 1)
            pool.memset(dummy[:, :], 0.0).then_inc(consts_done, 1)

            for kt in range(1, KT, 2):
                pool.wait_ge(h_hi_done, kt + 1)
                pool.tensor_tensor(h_lo[:, kt, :], xT[:, kt, :], h_hi[:, kt, :].bitcast(F32), ALU.subtract)\
                    .then_inc(h_lo_odd, 1)

            def split_lo(b, p):
                pool.wait_ge(w_hi, 4 * b + p + 1)
                pool.tensor_tensor(wr_lo[:, p, :, :], w_raw[:, p, :, :], wr_hi[:, p, :, :].bitcast(F32),
                                   ALU.subtract).then_inc(w_lo, 1)

            def split_ahead(b0, slot, last=False):
                if slot % 4 == 0:
                    at = slot // 4 + 2
                    if not (last and at >= 16):
                        split_lo(b0 + at // 4, at % 4)

            for p in range(4):
                split_lo(0, p)
            split_lo(1, 0)
            split_lo(1, 1)
            for slot in range(SLOTS):
                split_ahead(1, slot)

            def fox_mask(m, n):
                if n == 0:
                    pool.wait_ge(fox_bias_in, 16 * m + 16)
                else:
                    pool.wait_ge(fox_max, 8 * m + n)
                b = blk(f_bias, NB - 1 - n)
                pool.tensor_tensor(b, b, causal_fox[:, :], ALU.add).then_inc(fox_masked, 1)

            def part_B(m, last=False):
                for slot in range(SLOTS):
                    split_ahead(8 * m + B0, slot, last)
                    for n in range(NB):
                        if slot == fox_slot(n) - 4:
                            fox_mask(m, n)

            def gdn(m, slot):
                if slot == 10:
                    pool.wait_ge(gdn_att_mm, 2 * m + 2)
                    pool.wait_ge(gdn_decays, 3 * m + 3)
                    pool.tensor_tensor(gq[:, :], gq[:, :], g_dec, ALU.mult).then_inc(gdn_qe, 1)
                if slot == 12:
                    pool.wait_ge(gdn_n, 8 * m + 8)
                    pool.tensor_tensor(blocks(g_t), blocks(g_n), over_blocks(level[:, 0, :], NB), ALU.mult)\
                        .then_inc(gdn_t1, 1)
                    pool.wait_ge(gdn_t1, 2 * m + 1)
                    pool.tensor_tensor(blocks(g_t), blocks(g_t), over_blocks(ident[:, :], NB), ALU.add)\
                        .then_inc(gdn_t1, 1)

            def part_A(m):
                for slot in range(SLOTS):
                    split_ahead(8 * m + A0, slot)
                    gdn(m, slot)

            part_B(0)
            part_A(0)
            with pool.Fori(1, H - 1) as m:
                part_B(m)
                part_A(m)
            part_B(H - 1, last=True)

            def split_m(n, i, src):
                pool.wait_ge(m_hi_done, n + 1)
                pool.tensor_tensor(m_lo[:, i, :], src, m_hi[:, i, :].bitcast(F32), ALU.subtract)\
                    .then_inc(m_lo_done, 1)

            def split_wo(q, m):
                pool.wait_ge(wo_hi_done, q + 1)
                pool.tensor_tensor(wo_lo[:, m % 4, :], wo_raw[:, m % 4, :], wo_hi[:, m % 4, :].bitcast(F32),
                                   ALU.subtract).then_inc(wo_lo_done, 1)

            split_wo(0, 0)
            split_wo(1, 1)
            order = [i for i in range(2 * H - 1) if i != H - 1]
            for slot in range(SLOTS):
                gdn(H - 1, slot)
                if slot % 4 == 1 and slot // 4 < len(order):
                    n = slot // 4
                    split_m(n, order[n], [fq, fk][n % 2][:, :])
                if slot == 58:
                    split_m(len(order), H - 1, fz[:, :])
            split_m(len(order) + 1, 2 * H - 1, g_o)

            for idx in range(8):
                for m in range(KT):
                    q = idx * KT + m + 2
                    if q < 8 * KT:
                        split_wo(q, q % KT)
                    if idx and m in (2, 4, 6, 8):
                        add_x(pool, idx - 1, m // 2 - 1)
            for t in range(4):
                add_x(pool, 7, t)


        @block.tensor
        def _(pe):
            pe.wait_ge(consts_done, 1)
            banks = (mA, mB, mC, mD)
            pe.wait_ge(small_in, 16 * 10)
            pe.transpose(pair[1][:, 0:5 * KT + 3], rows_in[0:5 * KT + 3, 0, :], ident[0:5 * KT + 3, 0:5 * KT + 3])
            pe.transpose(pair[1][:, P:P + 3 * H * TAPS], rows_in[0:3 * H * TAPS, 1, :],
                         ident[0:3 * H * TAPS, 0:3 * H * TAPS]).then_inc(cols_turned, 1)
            for t in range(NB):
                pe.wait_ge(x_scaled, t + 1)
                for g in range(4):
                    if t:
                        pe.wait_ge(x_kept, 4 * (t - 1) + g + 1)
                    for i in range(4):
                        mm = pe.transpose(blk(banks[g], i), blk(x_in[:, t % 4, :], 4 * g + i), ident[:, :])
                    mm.then_inc(x_turned, 1)
            pe.wait_ge(ada_added, 2 * KT)
            for n in range(2 * KT):
                mm = pe.matmul(pair[0][:, n:n + 1], blk(acc[:, n // KT, :], n % KT), ones[:, 0:1],
                               start=True, stop=True)
            mm.then_inc(mod_summed, 1)

            def pair_taken(m, k0, n):
                if k0 == B0 and n < 2:
                    pe.wait_ge(fox_taken, 4 * m + 3 + n)
                elif k0 == B0:
                    pe.wait_ge(conv_tap, 9 * m + 3 * (n - 2) + 3)
                elif k0 == A0 and n == 0:
                    pe.wait_ge(conv_tap, 9 * m + 9)
                elif k0 == A0 and n == 1:
                    pe.wait_ge(gdn_z, m + 1)
                elif k0 == A0:
                    pe.wait_ge(fox_taken, 4 * m + 4 + n - 1)
                elif k0 == 1 and n == 1:
                    pe.wait_ge(gates_act, 2)
                elif k0 == 1 and n >= 2:
                    pe.wait_ge(fox_taken, n - 1)

            def project(m, k0, slot):
                n, kt = slot // KT, slot % KT
                p = kt // 4
                b = 8 * m + k0 + n
                to = pair[(k0 + n) % 2]
                if kt % 4 == 0:
                    pe.wait_ge(w_lo, 4 * b + p + 1)
                if kt == 0:
                    pair_taken(m, k0, n)
                if k0 == 0:
                    pe.wait_ge(h_lo_odd if kt % 2 else h_lo_even, kt // 2 + 1)
                hi, lo = wr_hi[:, p, kt % 4, :], wr_lo[:, p, kt % 4, :]
                for i, (w, h) in enumerate(((hi, h_hi), (hi, h_lo), (lo, h_hi))):
                    for g in range(2):
                        mm = pe.matmul(half(to, g), w, half(h[:, kt, :], g), start=(kt == 0 and i == 0),
                                       stop=(kt == KT - 1 and i == 2))
                if kt % 4 == 3:
                    mm.then_inc(w_used, 1)

            def column_sums(to, sq):
                for g in range(2):
                    mm = pe.matmul(to[g], ones[:, :], half(sq, g), start=True, stop=True)
                return mm

            def fox(m, slot):
                if slot == 1:
                    pe.wait_ge(fox_sq, 2 * m + 1)
                    column_sums((mA, mB), f_s[0]).then_inc(fox_ss, 1)
                if slot == 3:
                    pe.wait_ge(fox_sq, 2 * m + 2)
                    pe.wait_ge(fox_ln, 2 * m + 1)
                    column_sums((mA, mB), f_s[1]).then_inc(fox_ss, 1)
                if slot == 4:
                    pe.wait_ge(fox_taken, 4 * m + 4)
                    for g in range(2):
                        for j in range(4):
                            mm = pe.transpose(blk((mC, mD)[g], j), blk(vT[:, :], 4 * g + j), ident[:, :])
                        mm.then_inc(fox_vturn, 1)
                for n in range(NB):
                    i = NB - 1 - n
                    at = fox_slot(n)
                    if slot == at:
                        if n == 0:
                            pe.wait_ge(fox_ln, 2 * m + 2)
                            pe.wait_ge(fox_qk, 2 * m + 2)
                        else:
                            pe.wait_ge(fox_max, 8 * m + n)
                        for g in range(n_groups(n)):
                            keys = slice(g * HALF, min((g + 1) * HALF, (i + 1) * P))
                            mm = pe.matmul(mAB[:, keys], blk(fq[:, :], i), fk[:, keys], start=True, stop=True)
                        mm.then_inc(fox_scores, 1)
                    for g in range(n_groups(n)):
                        if slot == at + 4 + g:
                            if g == 0:
                                pe.wait_ge(fox_probs, 8 * m + n + 1)
                            if n == 0 and g == 0:
                                pe.wait_ge(fox_v, 2 * m + 2)
                            else:
                                pe.wait_ge(fox_pt, GROUPS * m + groups_before(n) + g)
                            for j in range(4 * g, min(4 * g + 4, i + 1)):
                                mm = pe.transpose(blk(mC, j % 4), blk(f_s[n % 2], j), ident[:, :])
                            mm.then_inc(fox_pturn, 1)
                    if slot == at + 6:
                        pe.wait_ge(fox_pt, GROUPS * m + groups_before(n + 1))
                        if n == 4:
                            pe.wait_ge(fox_half, 2 * m + 1)
                        for j in range(i + 1):
                            mm = pe.matmul(blk(mD, i % 4), fv[:, j, :], f_pt[:, j, :],
                                           start=(j == 0), stop=(j == i))
                        mm.then_inc(fox_pv, 1)

            def gdn(m, slot):
                if slot == 2:
                    pe.wait_ge(gdn_sq, 2 * m + 1)
                    column_sums((mA, mB), view(1)).then_inc(gdn_ss, 1)
                    pe.wait_ge(gdn_sq, 2 * m + 2)
                    column_sums((mC, mD), view(3)).then_inc(gdn_ss, 1)
                if slot == 5:
                    pe.wait_ge(gdn_ln, 2 * m + 1)
                    pe.wait_ge(conv_silu, 3 * m + 1)
                    for g in range(2):
                        for j in range(4):
                            mm = pe.transpose(blk((mA, mB)[g], j), blk(vT[:, :], 4 * g + j), ident[:, :])
                        mm.then_inc(gdn_vturn, 1)
                if slot == 6:
                    pe.wait_ge(gdn_ln, 2 * m + 2)
                    pe.wait_ge(gdn_qk, 2 * m + 2)
                    for g in range(2):
                        for j in range(4):
                            mm = pe.transpose(blk((mC, mD)[g], j), blk(gk[:, :], 4 * g + j), ident[:, :])
                        mm.then_inc(gdn_kturn, 1)
                if slot == 8:
                    pe.wait_ge(gdn_v, 2 * m + 2)
                    for g in range(2):
                        for j in range(4):
                            kb = blk(gk[:, :], 4 * g + j)
                            mm = pe.matmul(blk((mA, mB)[g], j), kb, kb, start=True, stop=True)
                        mm.then_inc(gdn_gram, 1)
                if slot == 9:
                    pe.wait_ge(gdn_kdec, 2 * m + 2)
                    for g in range(2):
                        for j in range(4):
                            mm = pe.matmul(blk((mC, mD)[g], j), blk(gk[:, :], 4 * g + j),
                                           blk(gq[:, :], 4 * g + j), start=True, stop=True)
                        mm.then_inc(gdn_att_mm, 1)
                if slot == 11:
                    pe.wait_ge(gdn_n, 8 * m + 8)
                    for g in range(2):
                        for j in range(4):
                            mm = pe.transpose(blk((mA, mB)[g], j), blk(g_n, 4 * g + j), ident[:, :])
                        mm.then_inc(gdn_nturn, 1)
                if slot == 13:
                    pe.wait_ge(gdn_t1, 2 * m + 2)
                    pe.wait_ge(gdn_att, 2 * m + 2)
                    for g in range(2):
                        for j in range(4):
                            mm = pe.transpose(blk((mC, mD)[g], j), blk(g_t, 4 * g + j), ident[:, :])
                        mm.then_inc(gdn_uturn, 1)
                L = LEVELS - 1
                for lv in range(1, LEVELS):
                    i = lv - 1
                    if slot == INV0 + 2 * i:
                        if i == 0:
                            pe.wait_ge(gdn_nt, 2 * m + 2)
                            pe.wait_ge(gdn_u1, 2 * m + 2)
                        else:
                            pe.wait_ge(inv_t_out, 2 * (L - 1) * m + 2 * i)
                            pe.wait_ge(inv_u_out, 2 * L * m + 2 * i)
                        for g in range(2):
                            for j in range(4):
                                mm = pe.matmul(blk((mA, mB)[g], j), blk(g_nt, 4 * g + j), blk(g_t, 4 * g + j),
                                               start=True, stop=True)
                            mm.then_inc(inv_p, 1)
                    if slot == INV0 + 2 * i + 1:
                        for g in range(2):
                            pe.wait_ge(inv_p_out, 2 * L * m + 2 * i + g + 1)
                            if lv < LEVELS - 1:
                                for j in range(4 * g, 4 * g + 4):
                                    mm = pe.matmul(blk((mC, mD)[g], j % 4), blk(g_u, j), blk(g_n, j),
                                                   start=True, stop=True)
                                mm.then_inc(inv_t, 1)
                            for j in range(4 * g, 4 * g + 4):
                                mm = pe.matmul(blk((mA, mB)[g], j % 4), blk(g_n, j), blk(g_u, j),
                                               start=True, stop=True)
                            mm.then_inc(inv_u, 1)
                for j in range(NB):
                    at = scan_slot(j)
                    if slot == at and j > 0:
                        pe.wait_ge(scan_state, 7 * m + j)
                        if j == 1:
                            pe.wait_ge(inv_u_out, 2 * L * m + 2 * L)
                        pe.matmul(mA[:, 0:P], blk(gk[:, :], j), state[j % 2], start=True, stop=True)\
                            .then_inc(scan_z, 1)
                    if slot == at + 1:
                        if j == 0:
                            pe.wait_ge(inv_u_out, 2 * L * m + 2 * L)
                            y_in = gv[:, 0, :]
                        else:
                            pe.wait_ge(scan_y, 7 * m + j)
                            y_in = ybuf[j % 2]
                        pe.matmul(mB[:, 0:P], blk(g_u, j), y_in, start=True, stop=True).then_inc(scan_v, 1)
                    if slot == at + 2:
                        pe.wait_ge(scan_vnew, 8 * m + j + 1)
                        if j < NB - 1:
                            pe.matmul(mC[:, 0:P], blk(g_kdec, j), vnew[j % 2], start=True, stop=True)\
                                .then_inc(scan_upd, 1)
                        if j == 0:
                            pe.wait_ge(gdn_qe, m + 1)
                        if j == 4:
                            pe.wait_ge(scan_o_out, 2 * m + 1)
                        if j > 0:
                            pe.matmul(blk(mD, j % 4), state[j % 2], blk(gq[:, :], j), start=True, stop=False)
                        pe.matmul(blk(mD, j % 4), vnew[j % 2], blk(g_att, j), start=(j == 0), stop=True)\
                            .then_inc(scan_o, 1)
                if slot == SLOTS - 4:
                    pe.wait_ge(out_sq, m + 1)
                    column_sums((mA, mB), g_t).then_inc(out_ss, 1)

            pe.wait_ge(mod_cols, 1)
            for slot in range(KT):
                project(0, 0, slot)
            for slot in range(SLOTS):
                project(0, 1, slot)
                if slot == 48:
                    pe.wait_ge(gates_dve, GATES_ROWS)
                    for j in range(NB):
                        mm = pe.transpose(blk(mAB, j)[:, 0:96], blk(gq[0:96, :], j), ident[0:96, 0:96])
                    mm.then_inc(gates_turned, 1)
                if slot == 58:
                    pe.wait_ge(gates_cols, 2)
                    pe.wait_ge(gate_added, KT)
                    for g in range(4):
                        mm = pe.matmul(ps[0:1, 4 + g, :], ones[:, 0:1], acc_gate[:, g * HALF:(g + 1) * HALF],
                                       start=True, stop=True)
                    mm.then_inc(gate_summed, 1)

            def part_B(m):
                for slot in range(SLOTS):
                    project(m, B0, slot)
                    fox(m, slot)

            def part_A(m):
                for slot in range(SLOTS):
                    project(m, A0, slot)
                    gdn(m, slot)

            part_B(0)
            part_A(0)
            with pe.Fori(1, H - 1) as m:
                part_B(m)
                part_A(m)
            part_B(H - 1)
            for slot in range(SLOTS):
                gdn(H - 1, slot)

            for idx in range(8):
                hf = idx // 4
                for mt in range(KT):
                    q = idx * KT + mt
                    pe.wait_ge(wo_lo_done, q + 1)
                    if q == 0:
                        pe.wait_ge(m_lo_done, 2 * H)
                    for t in range(4):
                        tok = slice((4 * hf + t) * P, (4 * hf + t + 1) * P)
                        if mt == 0 and idx >= 2:
                            pe.wait_ge(y_gated, 4 * (idx - 2) + t + 1)
                        to = ps[:, idx % 2 * 4 + t, :]
                        hi, lo = m_hi[:, mt, tok], m_lo[:, mt, tok]
                        for i, (a, w) in enumerate(((hi, wo_hi), (hi, wo_lo), (lo, wo_hi))):
                            mm = pe.matmul(to, a, w[:, mt % 4, :], start=(mt == 0 and i == 0),
                                           stop=(mt == KT - 1 and i == 2))
                        if mt == KT - 1:
                            mm.then_inc(y_ready, 1)
                        elif t == 3:
                            mm.then_inc(wo_used, 1)

        @block.scalar
        def _(act):
            for row, vec in ((0, c), (KT, norm_g), (2 * KT, b_ada), (5 * KT, fox_qn_g), (5 * KT + 1, fox_kn_g),
                             (5 * KT + 2, gdn_norm_g)):
                n = vec.shape[1] // P
                act.dma_start(rows_in[row:row + n, 0, :], vec.rearrange("a (t p) -> (a t) p", p=P)).then_inc(small_in, 16)
            act.dma_start(rows_in[0:3 * H * TAPS, 1, :], gdn_conv_w[0].rearrange("k (t p) -> (k t) p", p=P))\
                .then_inc(small_in, 16)
            act.wait_ge(gates_zeroed, 3)
            act.dma_start(gatecol[0:H, 1:2], b_fgate.rearrange("a h -> h a")).then_inc(small_in, 16)
            act.dma_start(gatecol[32:32 + H, 1:2], gdn_dt_bias.rearrange("a h -> h a")).then_inc(small_in, 16)
            act.dma_start(gatecol[32:32 + H, 2:3], gdn_A_log.rearrange("a h -> h a")).then_inc(small_in, 16)
            act.wait_ge(w_zeroed, 1)
            for to, col, n in ((0, COL_F, H), (32, COL_AB, 2 * H)):
                act.dma_start(w_raw[:, :, :, to:to + n].rearrange("p a b n -> p (a b) n"),
                              w_in_v[:, :, col:col + n]).then_inc(gates_w_in, 16)
            act.wait_ge(cols_ready, 1)
            act.activation(c_col, c_col, ACT.Silu).then_inc(silu_c, 1)
            act.wait_ge(consts, 7)
            for t in range(NB):
                act.wait_ge(x_loaded[t % 4], 16 * (t // 4 + 1))
                act.activation(junk[:, :], x_in[:, t % 4, :], ACT.Square, accum_out=xstat[:, t:t + 1])\
                    .then_inc(x_sq, 1)
                act.wait_ge(x_sq, t + 1)
                act.activation(xstat[:, 8 + t:9 + t], xstat[:, t:t + 1], ACT.Ln, bias=eps[:, :], scale=1.0 / D)\
                    .then_inc(x_ln, 1)
                act.wait_ge(x_ln, t + 1)
                act.activation(xstat[:, 16 + t:17 + t], xstat[:, 8 + t:9 + t], ACT.Exp, scale=-0.5)\
                    .then_inc(x_rstd, 1)
                if t:
                    keep(act, t - 1)
            keep(act, NB - 1)
            act.wait_ge(mod_cols, 1)
            act.wait_ge(x_kept, 4 * NB)
            for kt in range(KT):
                act.activation(xT[:, kt, :], xT[:, kt, :], ACT.Identity, bias=s_col[:, kt:kt + 1],
                               scale=a_col[:, kt:kt + 1]).then_inc(h_affine, 1)

            def split_hi(b, p, col=None):
                if b is None:
                    act.wait_ge(gates_w_put, 1)
                else:
                    act.wait_ge(w_loaded[p], 16 * b)
                    act.wait_ge(w_used, 4 * b + p - 3)
                act.activation(wr_hi[:, p, :, :], w_raw[:, p, :, :], ACT.Copy).then_inc(w_hi, 1)

            def split_ahead(b0, slot, last=False):
                if slot % 4 == 0:
                    at = slot // 4 + 2
                    if not (last and at >= 16):
                        split_hi(b0 + at // 4, at % 4)

            for p in range(4):
                split_hi(None, p)
            split_hi(1, 0)
            split_hi(1, 1)

            act.wait_ge(w_used, 4)
            act.wait_ge(gates_dve, 2)
            act.activation(gq[0:64, :], pair[0][0:64, :], ACT.Identity, bias=gatecol[0:64, 1:2],
                           scale=gatecol[0:64, 0:1]).then_inc(gates_act, 1)
            act.activation(gq[64:96, :], pair[0][64:96, :], ACT.Exp, scale=-1.0)\
                .then_inc(gates_act, 1)
            act.activation(gatecol[0:64, 2:3], gatecol[0:64, 2:3], ACT.Exp).then_inc(gates_act, 1)
            act.wait_ge(gates_act, 1)
            act.activation(gk[0:64, :], gq[0:64, :], ACT.Abs).then_inc(gates_act, 1)
            act.wait_ge(gates_act, 4)
            act.activation(gk[0:64, :], gk[0:64, :], ACT.Exp, scale=-1.0).then_inc(gates_act, 1)
            act.wait_ge(gates_dve, 3)
            act.activation(flatb(gv)[0:64, :], gz[0:64, :], ACT.Ln).then_inc(gates_act, 1)

            def take_fox(m, n, k0):
                b, used = 8 * m + k0 + n, (k0 + n) % 2
                act.wait_ge(w_used, 4 * b + 4)
                if k0 == A0 and n == 0:
                    act.wait_ge(fox_half, 2 * m + 2)
                if k0 == A0 and n == 2:
                    act.wait_ge(mixed_stored, 16 * (2 * m + 1))
                if k0 == A0 and n == 3:
                    act.wait_ge(inv_u, 2 * (LEVELS - 1) * m + 2 * (LEVELS - 1))
                to = (fq, fk, fz, vT)[n]
                act.activation(to[:, :], pair[used], ACT.Silu if n == 2 else ACT.Copy)\
                    .then_inc(fox_taken, 1)

            def take_gdn(m, n):
                b, used = 8 * m + B0 + n, (B0 + n) % 2
                act.wait_ge(w_used, 4 * b + 4)
                if n == 0:
                    act.wait_ge(fox_vturn, 2 * m + 2)
                    act.wait_ge(head_conv, m + 1)
                if n == 3:
                    act.activation(gz[:, :], pair[used], ACT.Silu).then_inc(gdn_z, 1)
                else:
                    act.activation((vT, gq, gk)[n][:, :], pair[used], ACT.Copy,
                                   scale=hconv[:, CONV_AT[n], TAPS - 1:TAPS]).then_inc(conv_first, 1)

            def silu_gdn(m, n):
                act.wait_ge(conv_tap, 9 * m + 3 * n + 3)
                t = (vT, gq, gk)[n]
                act.activation(t[:, :], t[:, :], ACT.Silu).then_inc(conv_silu, 1)

            def fox(m, slot):
                if slot == 0:
                    if not is_zero(m):
                        act.wait_ge(gdn_done, m)
                    for i, t in enumerate((fq, fk)):
                        act.wait_ge(fox_taken, 4 * m + 2 + 2 * i)
                        act.activation(f_s[i], t[:, :], ACT.Square).then_inc(fox_sq, 1)
                for i, at in enumerate((2, 4)):
                    if slot == at:
                        act.wait_ge(fox_ss, 2 * m + i + 1)
                        act.activation(f_s[i], mAB, ACT.Ln, bias=eps[:, :], scale=1.0 / HD).then_inc(fox_ln, 1)
                        act.wait_ge(fox_ln, 2 * m + i + 1)
                        act.activation(f_s[i], f_s[i], ACT.Exp, scale=-0.5).then_inc(fox_rstd, 1)
                for n in range(NB):
                    if slot == fox_slot(n) + 2:
                        s = f_s[n % 2][:, 0:(NB - n) * P]
                        act.wait_ge(fox_max, 8 * m + n + 1)
                        act.activation(s, s, ACT.Exp, bias=negmax[:, n:n + 1], scale=-1.0,
                                       accum_out=lsum[:, n:n + 1]).then_inc(fox_exp, 1)

            def gdn(m, slot):
                if slot == 0:
                    act.wait_ge(fox_half, 2 * m + 2)
                    act.wait_ge(conv_silu, 3 * m + 3)
                    act.activation(view(1), gq[:, :], ACT.Square).then_inc(gdn_sq, 1)
                    act.activation(view(3), gk[:, :], ACT.Square).then_inc(gdn_sq, 1)
                if slot in (2, 3):
                    i = slot - 2
                    act.wait_ge(gdn_ss, 2 * m + i + 1)
                    to = (view(1), view(3))[i]
                    act.activation(to, (mAB, flat(ps[:, 6:8, :]))[i], ACT.Ln, bias=eps[:, :]).then_inc(gdn_ln, 1)
                    act.wait_ge(gdn_ln, 2 * m + i + 1)
                    act.activation(to, to, ACT.Exp, scale=-0.5).then_inc(gdn_rstd, 1)
                if slot == 4:
                    act.wait_ge(gdn_cols, 4 * m + 2)
                    act.activation(edl[:, :], edl[:, :], ACT.Exp).then_inc(gdn_cexp, 1)
                    act.activation(eg[:, :], hcol[:, 0:NB], ACT.Exp).then_inc(gdn_cexp, 1)
                if slot == 6:
                    act.wait_ge(gdn_args, 16 * m + 16)
                    act.activation(g_t, g_t, ACT.Exp, scale=-1.0).then_inc(gdn_decays, 1)
                    act.activation(g_att, g_att, ACT.Exp).then_inc(gdn_decays, 1)
                    act.activation(g_dec, g_dec, ACT.Exp).then_inc(gdn_decays, 1)
                if slot == 11:
                    if not is_zero(m):
                        act.wait_ge(mixed_stored, 16 * (2 * m + 1))
                    for g in range(2):
                        act.wait_ge(gdn_nturn, 2 * m + g + 1)
                        act.activation(half(g_nt, g), (mA, mB)[g], ACT.Copy).then_inc(gdn_nt, 1)
                if slot == 13:
                    for g in range(2):
                        act.wait_ge(gdn_uturn, 2 * m + g + 1)
                        act.activation(half(g_u, g), (mC, mD)[g], ACT.Copy).then_inc(gdn_u1, 1)
                for j in range(NB):
                    if slot == scan_slot(j) + 1:
                        act.wait_ge(scan_v, 8 * m + j + 1)
                        act.activation(vnew[j % 2], mB[:, 0:P], ACT.Copy).then_inc(scan_vnew, 1)
                    if slot == scan_slot(j) + 2 and j in (3, 7):
                        act.wait_ge(scan_o, 8 * m + j + 1)
                        act.activation(half(g_o, j // 4), mD, ACT.Copy).then_inc(scan_o_out, 1)
                if slot == SLOTS - 4:
                    act.wait_ge(scan_o_out, 2 * m + 2)
                    act.activation(g_t, g_o, ACT.Square).then_inc(out_sq, 1)
                    act.wait_ge(out_ss, m + 1)
                    act.activation(g_t, mAB, ACT.Ln, bias=eps[:, :], scale=1.0 / HD).then_inc(out_ln, 1)
                    act.wait_ge(out_ln, m + 1)
                    act.activation(g_t, g_t, ACT.Exp, scale=-0.5).then_inc(out_rstd, 1)

            for slot in range(SLOTS):
                split_ahead(1, slot)
                if slot in (16, 32, 48):
                    take_fox(0, slot // KT - 1, 1)
            take_fox(0, 3, 1)
            act.wait_ge(rows_stored, 32)
            act.wait_ge(gates_turned, 1)
            act.wait_ge(gate_stored, 16)

            def part_B(m, last=False):
                for slot in range(SLOTS):
                    split_ahead(8 * m + B0, slot, last)
                    fox(m, slot)
                    if slot in (16, 32, 48):
                        take_gdn(m, slot // KT - 1)
                    if slot in (22, 38, 54):
                        silu_gdn(m, slot // KT - 1)
                take_gdn(m, 3)

            def part_A(m):
                for slot in range(SLOTS):
                    split_ahead(8 * m + A0, slot)
                    gdn(m, slot)
                    if slot in (16, 32, 48):
                        take_fox(m, slot // KT - 1, A0)
                take_fox(m, 3, A0)

            part_B(0)
            part_A(0)
            with act.Fori(1, H - 1) as m:
                part_B(m)
                part_A(m)
            part_B(H - 1, last=True)

            def split_m(n, i, src):
                act.activation(m_hi[:, i, :], src, ACT.Copy).then_inc(m_hi_done, 1)

            def split_wo(q):
                act.wait_ge(wo_loaded[q % 4], 16 * (q // 4 + 1))
                if q >= 4 and (q - 4) % KT == KT - 1:
                    act.wait_ge(y_ready, 4 * ((q - 4) // KT) + 4)
                elif q >= 4:
                    act.wait_ge(wo_used, (KT - 1) * ((q - 4) // KT) + (q - 4) % KT + 1)
                act.activation(wo_hi[:, q % 4, :], wo_raw[:, q % 4, :], ACT.Copy).then_inc(wo_hi_done, 1)

            act.wait_ge(w_used, 4 * (8 * H + 1))
            split_wo(0)
            split_wo(1)
            order = [i for i in range(2 * H - 1) if i != H - 1]
            for slot in range(SLOTS):
                gdn(H - 1, slot)
                if slot % 4 == 1 and slot // 4 < len(order):
                    n = slot // 4
                    act.wait_ge(m_loaded[n % 2], 16 * (n // 2 + 1))
                    split_m(n, order[n], [fq, fk][n % 2][:, :])
                if slot == 58:
                    split_m(len(order), H - 1, fz[:, :])
            act.wait_ge(gdn_done, H)
            split_m(len(order) + 1, 2 * H - 1, g_o)

            def finish(idx, t):
                hf, ch = idx // 4, idx % 4
                act.wait_ge(y_added, 4 * idx + t + 1)
                act.activation(sq_out[:, 0, :], y[:, t, ch * HALF:(ch + 1) * HALF], ACT.Square,
                               accum_out=xstat[:, 4 * t + ch:4 * t + ch + 1]).then_inc(y_sq, 1)
                if ch == 3:
                    k = 4 * hf + t
                    act.wait_ge(y_sum, k + 1)
                    act.activation(xstat[:, 20 + t:21 + t], xstat[:, 16 + t:17 + t], ACT.Ln, bias=eps[:, :],
                                   scale=1.0 / D).then_inc(y_ln, 1)
                    act.wait_ge(y_ln, k + 1)
                    act.activation(xstat[:, 24 + t:25 + t], xstat[:, 20 + t:21 + t], ACT.Exp, scale=-0.5)\
                        .then_inc(y_rstd, 1)

            for idx in range(8):
                for mt in range(KT):
                    q = idx * KT + mt + 2
                    if q < 8 * KT:
                        split_wo(q)
                    if idx and mt in (3, 5, 7, 9):
                        finish(idx - 1, (mt - 3) // 2)
            for t in range(4):
                finish(7, t)

        @block.vector
        def _(dve):
            dve.wait_ge(cols_turned, 1)
            dve.tensor_copy(cols[:, :], pair[1][:, 0:5 * KT + 3]).then_inc(cols_ready, 1)
            dve.tensor_copy(convw[:, :], pair[1][:, P:P + 3 * H * TAPS]).then_inc(cols_ready, 1)
            dve.wait_ge(silu_c, 1)
            for n in range(2 * KT):
                kt, part = n // 2, n % 2
                dve.wait_ge(ada_loaded[n % 6], 16 * (n // 6 + 1))
                if kt == 0:
                    dve.tensor_scalar(acc[:, part, :], ada[:, n % 6, :], c_col[:, kt:kt + 1], None, ALU.mult)\
                        .then_inc(ada_added, 1)
                else:
                    dve.wait_ge(ada_added, n - 1)
                    dve.scalar_tensor_tensor(out=acc[:, part, :], in0=ada[:, n % 6, :], scalar=c_col[:, kt:kt + 1],
                                             in1=acc[:, part, :], op0=ALU.mult, op1=ALU.add).then_inc(ada_added, 1)
                if n % 3 == 1 and n // 3 < NB:
                    scale_x(dve, n // 3)
            dve.wait_ge(mod_summed, 1)
            dve.tensor_tensor(mod[:, :], pair[0][:, 0:2 * KT], b_col[:, 0:2 * KT], ALU.add).then_inc(mod_biased, 1)
            dve.wait_ge(mod_biased, 1)
            dve.tensor_copy(s_col[:, :], mod[:, 0:KT]).then_inc(mod_biased, 1)
            dve.wait_ge(mod_biased, 2)
            dve.scalar_tensor_tensor(out=a_col[:, :], in0=mod[:, KT:2 * KT], scalar=1.0, in1=g_col,
                                     op0=ALU.add, op1=ALU.mult).then_inc(mod_cols, 1)
            dve.wait_ge(gates_zeroed, 3)
            dve.tensor_tensor(gatecol[:, 1:2], gatecol[:, 1:2], gatecol[:, 0:1], ALU.mult).then_inc(gates_dve, 1)
            dve.tensor_scalar(qgain, qgain, SCALE, None, ALU.mult).then_inc(gates_dve, 1)
            for kt in range(KT):
                dve.wait_ge(h_affine, kt + 1)
                dve.tensor_copy(h_hi[:, kt, :], xT[:, kt, :]).then_inc(h_hi_done, 1)
                if kt % 2 == 0:
                    dve.wait_ge(h_hi_done, kt + 1)
                    dve.tensor_tensor(h_lo[:, kt, :], xT[:, kt, :], h_hi[:, kt, :].bitcast(F32), ALU.subtract)\
                        .then_inc(h_lo_even, 1)

            r, e, w, ln = gq[0:64, :], gk[0:64, :], gz[0:64, :], flatb(gv)[0:64, :]
            done = [2]

            def step(ins):
                ins.then_inc(gates_dve, 1)
                done[0] += 1
                dve.wait_ge(gates_dve, done[0])

            dve.wait_ge(gates_act, 5)
            step(dve.tensor_scalar(w, e, 1.0, None, ALU.add))
            dve.wait_ge(gates_act, 6)
            step(dve.scalar_tensor_tensor(out=e, in0=w, scalar=-1.0, in1=e, op0=ALU.add, op1=ALU.subtract))
            step(dve.reciprocal(w, w))
            step(dve.scalar_tensor_tensor(out=e, in0=e, scalar=-1.0, in1=w, op0=ALU.mult, op1=ALU.mult))
            step(dve.tensor_tensor(ln, ln, e, ALU.add))
            step(dve.scalar_tensor_tensor(out=r, in0=r, scalar=0.0, in1=ln, op0=ALU.max, op1=ALU.add))
            step(dve.scalar_tensor_tensor(out=gatecol[0:64, 3:4], in0=gatecol[0:64, 2:3], scalar=-1.0,
                                          in1=gatecol[0:64, 0:1], op0=ALU.mult, op1=ALU.mult))
            step(dve.tensor_scalar(r, r, gatecol[0:64, 3:4], None, ALU.mult))
            step(dve.tensor_tensor_scan(gq[0:H, :], ones[0:H, 0:1].to_broadcast([H, SEQ]), gq[0:H, :], 0.0,
                                        ALU.mult, ALU.add))
            for j in range(NB):
                g = blk(gq[32:32 + H, :], j)
                step(dve.tensor_tensor_scan(g, ones[32:32 + H, 0:1].to_broadcast([H, P]), g, 0.0,
                                            ALU.mult, ALU.add))
            step(dve.tensor_scalar(gq[64:96, :], gq[64:96, :], 1.0, None, ALU.add))
            step(dve.reciprocal(gq[64:96, :], gq[64:96, :]))
            assert done[0] == GATES_ROWS
            for kt in range(KT):
                dve.wait_ge(gate_loaded[kt % 2], 16 * (kt // 2 + 1))
                if kt == 0:
                    dve.tensor_scalar(acc_gate, ada_gate[0], c_col[:, 0:1], None, ALU.mult).then_inc(gate_added, 1)
                else:
                    dve.wait_ge(gate_added, kt)
                    dve.scalar_tensor_tensor(out=acc_gate, in0=ada_gate[kt % 2], scalar=c_col[:, kt:kt + 1],
                                             in1=acc_gate, op0=ALU.mult, op1=ALU.add).then_inc(gate_added, 1)
            dve.wait_ge(gates_turned, 1)
            for i, row in enumerate((32, 64)):
                src = blocks(mAB)[:, :, row:row + H].rearrange("p j h -> p h j")
                dve.tensor_copy(gcol[:, :, i * NB:(i + 1) * NB], src).then_inc(gates_cols, 1)
            dve.wait_ge(gate_summed, 1)
            dve.wait_ge(gate_biased, 16)
            dve.tensor_tensor(ada_gate[1][0:1, :], flat(ps[0:1, 4:8, :]), ada_gate[0][0:1, :], ALU.add)\
                .then_inc(gate_row, 1)
            dve.wait_ge(gates_cols, 2)

            def conv_tap_of(m, n, i):
                used = (B0 + n) % 2
                t = (vT, gq, gk)[n][:, i:SEQ]
                if i == 1:
                    dve.wait_ge(conv_first, 3 * m + n + 1)
                else:
                    dve.wait_ge(conv_tap, 9 * m + 3 * n + i - 1)
                dve.scalar_tensor_tensor(out=t, in0=pair[used][:, 0:SEQ - i],
                                         scalar=hconv[:, CONV_AT[n], TAPS - 1 - i:TAPS - i], in1=t,
                                         op0=ALU.mult, op1=ALU.add).then_inc(conv_tap, 1)

            def fox(m, slot):
                if slot == 0:
                    dve.tensor_copy(hconv[:, :, :], convw[:, :].rearrange("p (k s h) -> p s k h", k=TAPS, s=3)
                                    [:, :, :, bass.ds(m, 1)].rearrange("p s k o -> p s (k o)"))\
                        .then_inc(head_conv, 1)
                for i, (at, t, gain) in enumerate(((3, fq, qgain), (5, fk, kgain))):
                    if slot == at:
                        dve.wait_ge(fox_rstd, 2 * m + i + 1)
                        dve.scalar_tensor_tensor(out=t[:, :], in0=t[:, :], scalar=gain, in1=f_s[i],
                                                 op0=ALU.mult, op1=ALU.mult).then_inc(fox_qk, 1)
                if slot == 5:
                    for g in range(2):
                        dve.wait_ge(fox_vturn, 2 * m + g + 1)
                        dve.tensor_copy(fv[:, 4 * g:4 * g + 4, :], blocks((mC, mD)[g], 4)).then_inc(fox_v, 1)
                for n in range(NB):
                    i = NB - 1 - n
                    at = fox_slot(n)
                    L = (i + 1) * P
                    s = f_s[n % 2][:, 0:L]
                    if slot == at + 1:
                        dve.wait_ge(fox_scores, 8 * m + n + 1)
                        dve.wait_ge(fox_masked, 8 * m + n + 1)
                        if n >= 2:
                            dve.wait_ge(fox_pturn, GROUPS * m + groups_before(n - 1))
                        dve.memset(dummy[:, :], 0.0)
                        dve.tensor_tensor_reduce(s, mAB[:, 0:L], f_bias[:, 0:L], -1.0, BIG, ALU.add, ALU.min,
                                                 negmax[:, n:n + 1]).then_inc(fox_max, 1)
                    if slot == at + 3:
                        dve.wait_ge(fox_exp, 8 * m + n + 1)
                        dve.reciprocal(rsum[:, n:n + 1], lsum[:, n:n + 1]).then_inc(fox_recip, 1)
                        dve.wait_ge(fox_recip, 8 * m + n + 1)
                        dve.tensor_scalar(s, s, rsum[:, n:n + 1], None, ALU.mult).then_inc(fox_probs, 1)
                    for g in range(n_groups(n)):
                        if slot == at + 4 + g:
                            k = min(4, i + 1 - 4 * g)
                            dve.wait_ge(fox_pturn, GROUPS * m + groups_before(n) + g + 1)
                            if n and g == 0:
                                dve.wait_ge(fox_pv, 8 * m + n)
                            dve.tensor_copy(f_pt[:, 4 * g:4 * g + k, :], blocks(mC, 4)[:, 0:k, :]).then_inc(fox_pt, 1)
                    if slot == at + 6 and n in (3, 7):
                        hv = half(fz[:, :], 1 if n == 3 else 0)
                        dve.wait_ge(fox_pv, 8 * m + n + 1)
                        dve.tensor_tensor(hv, mD, hv, ALU.mult).then_inc(fox_half, 1)

            def gdn(m, slot):
                if slot == 0:
                    dve.tensor_copy(hcol[:, :], gcol[:, bass.ds(m, 1), :].rearrange("p o k -> p (o k)"))\
                        .then_inc(gdn_cols, 1)
                    dve.wait_ge(gdn_cols, 4 * m + 1)
                    dve.wait_ge(dec_in, 16 * m + 16)
                    last = g_dec.rearrange("p (b q) -> p q b", q=P)[:, P - 1, :]
                    dve.tensor_tensor(edl[:, :], last, hcol[:, 0:NB], ALU.subtract).then_inc(gdn_cols, 1)
                    dve.tensor_scalar(negbeta[:, :], hcol[:, NB:], -1.0, None, ALU.mult).then_inc(gdn_cols, 1)
                    for j in range(NB):
                        dve.scalar_tensor_tensor(out=blk(g_t, j), in0=blk(g_dec, j), scalar=hcol[:, j:j + 1],
                                                 in1=strict[:, :], op0=ALU.subtract, op1=ALU.add)\
                            .then_inc(gdn_args, 1)
                if slot == 3:
                    for j in range(NB):
                        dve.scalar_tensor_tensor(out=blk(g_att, j), in0=blk(g_dec, j), scalar=hcol[:, j:j + 1],
                                                 in1=causal_t[:, :], op0=ALU.subtract, op1=ALU.add)\
                            .then_inc(gdn_args, 1)
                if slot in (4, 5):
                    i = slot - 4
                    t, rs = ((gq, view(1)), (gk, view(3)))[i]
                    dve.wait_ge(gdn_rstd, 2 * m + i + 1)
                    dve.scalar_tensor_tensor(out=t[:, :], in0=t[:, :], scalar=(SCALE, 1.0)[i], in1=rs,
                                             op0=ALU.mult, op1=ALU.mult).then_inc(gdn_qk, 1)
                if slot == 5:
                    dve.wait_ge(gdn_cexp, 2 * m + 2)
                    dve.wait_ge(gdn_cols, 4 * m + 3)
                    dve.tensor_tensor(negbg[:, :], eg[:, :], negbeta[:, :], ALU.mult).then_inc(gdn_cols, 1)
                if slot == 6:
                    for g in range(2):
                        dve.wait_ge(gdn_vturn, 2 * m + g + 1)
                        dve.tensor_tensor(gv[:, 4 * g:4 * g + 4, :], blocks((mA, mB)[g], 4),
                                          spread(hcol[:, NB + 4 * g:NB + 4 * g + 4], 4), ALU.mult).then_inc(gdn_v, 1)
                if slot == 7:
                    for g in range(2):
                        dve.wait_ge(gdn_kturn, 2 * m + g + 1)
                        dve.tensor_tensor(blocks(half(g_kdec, g), 4), blocks((mC, mD)[g], 4),
                                          spread(edl[:, 4 * g:4 * g + 4], 4), ALU.mult).then_inc(gdn_kdec, 1)
                if slot == 9:
                    dve.wait_ge(gdn_decays, 3 * m + 1)
                    for j in range(NB):
                        dve.wait_ge(gdn_gram, 2 * m + j // 4 + 1)
                        dve.scalar_tensor_tensor(out=blk(g_n, j), in0=blk(mAB, j), scalar=negbeta[:, j:j + 1],
                                                 in1=blk(g_t, j), op0=ALU.mult, op1=ALU.mult).then_inc(gdn_n, 1)
                if slot == 10:
                    dve.wait_ge(gdn_decays, 3 * m + 2)
                    for g in range(2):
                        dve.wait_ge(gdn_att_mm, 2 * m + g + 1)
                        dve.tensor_tensor(half(g_att, g), (mC, mD)[g], half(g_att, g), ALU.mult).then_inc(gdn_att, 1)
                L = LEVELS - 1
                for lv in range(1, LEVELS):
                    i = lv - 1
                    if slot == INV0 + 2 * i:
                        for g in range(2):
                            dve.wait_ge(inv_p, 2 * L * m + 2 * i + g + 1)
                            dve.tensor_tensor(blocks(half(g_n, g), 4), blocks((mA, mB)[g], 4),
                                              over_blocks(level[:, lv, :], 4), ALU.mult).then_inc(inv_p_out, 1)
                    if slot == INV0 + 2 * i + 1:
                        for g in range(2):
                            if lv < LEVELS - 1:
                                dve.wait_ge(inv_t, 2 * (L - 1) * m + 2 * i + g + 1)
                                dve.tensor_tensor(half(g_t, g), (mC, mD)[g], half(g_t, g), ALU.add)\
                                    .then_inc(inv_t_out, 1)
                            dve.wait_ge(inv_u, 2 * L * m + 2 * i + g + 1)
                            dve.tensor_tensor(half(g_u, g), (mA, mB)[g], half(g_u, g), ALU.add)\
                                .then_inc(inv_u_out, 1)
                for j in range(NB):
                    at = scan_slot(j)
                    if slot == at and j > 0:
                        dve.wait_ge(scan_z, 7 * m + j)
                        dve.scalar_tensor_tensor(out=ybuf[j % 2], in0=mA[:, 0:P], scalar=negbg[:, j:j + 1],
                                                 in1=gv[:, j, :], op0=ALU.mult, op1=ALU.add).then_inc(scan_y, 1)
                    if slot == at + 2 and j < NB - 1:
                        dve.wait_ge(scan_upd, 7 * m + j + 1)
                        if j == 0:
                            dve.tensor_copy(state[1], mC[:, 0:P]).then_inc(scan_state, 1)
                        else:
                            dve.wait_ge(scan_state, 7 * m + j)
                            dve.scalar_tensor_tensor(out=state[(j + 1) % 2], in0=state[j % 2],
                                                     scalar=g_dec[:, j * P + P - 1:j * P + P], in1=mC[:, 0:P],
                                                     op0=ALU.mult, op1=ALU.add).then_inc(scan_state, 1)
                if slot == SLOTS - 3:
                    dve.wait_ge(out_rstd, m + 1)
                    dve.scalar_tensor_tensor(out=g_o, in0=g_o, scalar=ngain, in1=g_t,
                                             op0=ALU.mult, op1=ALU.mult).then_inc(out_norm, 1)
                    dve.wait_ge(gdn_z, m + 1)
                    dve.wait_ge(out_norm, m + 1)
                    dve.tensor_tensor(g_o, g_o, gz[:, :], ALU.mult).then_inc(gdn_done, 1)

            def part_B(m):
                for slot in range(SLOTS):
                    fox(m, slot)
                    for n in range(3):
                        for i in range(1, TAPS):
                            if slot == KT * (n + 1) + i:
                                conv_tap_of(m, n, i)

            def part_A(m):
                for slot in range(SLOTS):
                    gdn(m, slot)

            part_B(0)
            part_A(0)
            with dve.Fori(1, H - 1) as m:
                part_B(m)
                part_A(m)
            part_B(H - 1)
            part_A(H - 1)

            dve.wait_ge(tail_rows_in, 32)
            for idx in range(8):
                hf, ch = idx // 4, idx % 4
                for t in range(4):
                    dve.wait_ge(y_ready, 4 * idx + t + 1)
                    if idx:
                        dve.wait_ge(y_added, 4 * (idx - 1) + t + 1)
                    dve.tensor_tensor(gated[:, t, :], ps[:, idx % 2 * 4 + t, :],
                                      gate_all[:, ch * HALF:(ch + 1) * HALF], ALU.mult).then_inc(y_gated, 1)
                if ch == 3:
                    for t in range(4):
                        k = 4 * hf + t
                        dve.wait_ge(y_sq, 4 * idx + t + 1)
                        dve.tensor_reduce(xstat[:, 16 + t:17 + t], xstat[:, 4 * t:4 * t + 4],
                                          mybir.AxisListType.X, ALU.add).then_inc(y_sum, 1)
                        dve.wait_ge(y_rstd, k + 1)
                        dve.scalar_tensor_tensor(out=y[:, t, :], in0=y[:, t, :], scalar=xstat[:, 24 + t:25 + t],
                                                 in1=fg_all[:, :], op0=ALU.mult, op1=ALU.mult).then_inc(y_done, 1)


_INS = ['x', 'c', 'norm_g', 'w_ada', 'b_ada', 'w_in', 'b_fgate', 'fox_qn_g', 'fox_kn_g',
        'gdn_conv_w', 'gdn_A_log', 'gdn_dt_bias', 'gdn_norm_g', 'w_out', 'final_g']


def kernel(**inputs):
    import numpy as _np
    import concourse.bacc as _bacc
    from concourse import mybir as _mybir
    from concourse.bass_utils import run_bass_kernel_spmd as _run

    nc = _bacc.Bacc("TRN2", target_bir_lowering=False, num_devices=1, dynamic_dma_scratch_size=1024)
    arrays, args = {}, []
    for name in _INS:
        a = _np.ascontiguousarray(inputs[name])
        arrays[f"in_{name}_dram"] = a
        args.append(nc.dram_tensor(f"in_{name}_dram", a.shape, _mybir.dt.from_np(a.dtype), kind="ExternalInput").ap())
    shape = inputs['x'].shape
    args.append(nc.dram_tensor("out_0_dram", shape, _mybir.dt.float32, kind="ExternalOutput").ap())
    hybrid_block(nc, *args)
    r = _run(nc, [arrays], core_ids=[0])
    return r.results[0]["out_0_dram"]
```

```python
from contextlib import ExitStack

import numpy as np
import concourse.bass as bass
from concourse import mybir

ALU = mybir.AluOpType
ACT = mybir.ActivationFunctionType
F32 = mybir.dt.float32
F32R = mybir.dt.float32r
BF16 = mybir.dt.bfloat16

P = 128
BIG = 3.0e38
EPS = 1e-6


def hybrid_block(nc, x, c, norm_g, w_ada, b_ada, w_in, b_fgate, fox_qn_g, fox_kn_g,
                 gdn_conv_w, gdn_A_log, gdn_dt_bias, gdn_norm_g, w_out, final_g, out):
    SEQ, D = x.shape[1], x.shape[2]
    H = b_fgate.shape[1]
    HD = fox_qn_g.shape[1]
    TAPS = gdn_conv_w.shape[1]
    KT = D // P
    NB = SEQ // P
    HALF = 512
    assert SEQ == 2 * HALF and HD == P and H == 8 and KT == 16 and TAPS == 4
    FW = H * HD
    SCALE = float(HD) ** -0.5
    SLOTS = 4 * KT
    COL_F = FW * 4
    COL_G = FW * 4 + H
    COL_AB = COL_G + 4 * FW
    FOX_COL = (0, FW, 3 * FW, 2 * FW)
    GDN_COL = (COL_G + 2 * FW, COL_G, COL_G + FW, COL_G + 3 * FW)
    CONV_AT = (2, 0, 1)
    LEVELS = 7

    xs = x[0]
    outs = out[0]
    w_in_v = w_in[0].rearrange("(t p) n -> p t n", p=P)
    w_out_v = w_out[0].rearrange("(t p) n -> p t n", p=P)
    w_ada_v = w_ada[0].rearrange("(t p) n -> p t n", p=P)

    rows_dram = nc.dram_tensor("rows_scratch", (2, H, SEQ), F32, kind="Internal").ap()
    rows_dram_flat = rows_dram.rearrange("g h t -> (g h) t")
    mixed_dram = nc.dram_tensor("mixed_scratch", (2 * H, P, SEQ), F32, kind="Internal").ap()
    gate_dram = nc.dram_tensor("gate_scratch", (1, D), F32, kind="Internal").ap()

    with ExitStack() as ctx:
        def sb(name, shape, dt=F32, stack=ctx):
            return stack.enter_context(nc.sbuf_tensor(name, shape, dt))

        def sem(name):
            return ctx.enter_context(nc.semaphore(name))

        ps = ctx.enter_context(nc.psum_tensor("ps", [P, 8, HALF], F32))

        def flat(ap):
            return ap.rearrange("p a b -> p (a b)")

        pair = [flat(ps[:, 0:2, :]), flat(ps[:, 2:4, :])]
        mAB = flat(ps[:, 4:6, :])
        mCD = flat(ps[:, 6:8, :])
        mA, mB, mC, mD = (ps[:, i, :] for i in (4, 5, 6, 7))

        eps = sb("eps", [P, 1])
        dummy = sb("dve_dummy", [P, 1])
        xstat = sb("xstat", [P, 32])
        cols = sb("cols", [P, 5 * KT + 3])
        c_col, g_col, b_col = cols[:, 0:KT], cols[:, KT:2 * KT], cols[:, 2 * KT:5 * KT]
        qgain, kgain, ngain = (cols[:, 5 * KT + i:5 * KT + i + 1] for i in range(3))
        a_col = sb("a_col", [P, KT])
        s_col = sb("s_col", [P, KT])
        mod = sb("mod", [P, 2 * KT])
        gatecol = sb("gatecol", [P, 4])
        hconv = sb("hconv", [P, 3, TAPS])
        hcol = sb("hcol", [P, 2 * NB])
        negbeta = sb("negbeta", [P, NB])
        negbg = sb("negbg", [P, NB])
        edl = sb("edl", [P, NB])
        eg = sb("eg", [P, NB])
        negmax = sb("negmax", [P, NB])
        lsum = sb("lsum", [P, NB])
        rsum = sb("rsum", [P, NB])
        ident = sb("ident", [P, P])
        ones = sb("ones", [P, P])
        causal_fox = sb("causal_fox", [P, P])
        causal_t = sb("causal_t", [P, P])
        strict = sb("strict", [P, P])
        level = sb("level", [P, LEVELS, P], BF16)
        lower_row = sb("lower_row", [P, LEVELS])
        gcol = sb("gcol", [P, H, 2 * NB])
        convw = sb("convw", [P, TAPS * 3 * H])

        begin = ExitStack()
        x_in = sb("x_in", [P, 4, D], F32, begin)
        ada = sb("ada", [P, 6, D], F32, begin)
        acc = sb("acc", [P, 2, D], F32, begin)
        junk = sb("junk", [P, D], F32, begin)
        rows_in = sb("rows_in", [P, 2, P], F32, begin)
        sb("begin_pad", [P, 2 * KT * SEQ - 13 * D - 2 * P], F32, begin)
        xT = sb("xT", [P, KT, SEQ], F32, begin)
        begin.close()

        main = ExitStack()
        h_hi = sb("h_hi", [P, KT, SEQ], F32R, main)
        h_lo = sb("h_lo", [P, KT, SEQ], F32R, main)
        fq = sb("fq", [P, SEQ], F32, main)
        fk = sb("fk", [P, SEQ], F32, main)
        fv = sb("fv", [P, NB, P], F32, main)
        fz = sb("fz", [P, SEQ], F32, main)
        gq = sb("gq", [P, SEQ], F32, main)
        gk = sb("gk", [P, SEQ], F32, main)
        gv = sb("gv", [P, NB, P], F32, main)
        gz = sb("gz", [P, SEQ], F32, main)
        vT = sb("vT", [P, SEQ], F32, main)
        scr = sb("scr", [P, 6 * SEQ], F32, main)
        small = sb("small", [P, 6, P], F32, main)
        sb("main_pad", [P, KT * SEQ - 15 * SEQ - 6 * P], F32, main)
        wr_hi = sb("wr_hi", [P, 4, 4, P], F32R, main)
        wr_lo = sb("wr_lo", [P, 4, 4, P], F32R, main)
        w_raw = sb("w_raw", [P, 4, 4, P], F32, main)
        main.close()

        tail = ExitStack()
        m_hi = sb("m_hi", [P, KT, SEQ], F32R, tail)
        m_lo = sb("m_lo", [P, KT, SEQ], F32R, tail)
        y = sb("y", [P, 4, D], F32, tail)
        gate_all = sb("gate_all", [P, D], F32, tail)
        fg_all = sb("fg_all", [P, D], F32, tail)
        gated = sb("gated", [P, 4, HALF], F32, tail)
        sq_out = sb("sq_out", [P, 2, HALF], F32, tail)
        sb("tail_pad", [P, KT * SEQ - 6 * D - 6 * HALF], F32, tail)
        wo_hi = sb("wo_hi", [P, 4, HALF], F32R, tail)
        wo_lo = sb("wo_lo", [P, 4, HALF], F32R, tail)
        wo_raw = sb("wo_raw", [P, 4, HALF], F32, tail)
        tail.close()

        def flatb(t):
            return t[:, :, :].rearrange("p b q -> p (b q)")

        def view(i, n=1):
            return scr[:, i * SEQ:(i + n) * SEQ]

        f_bias, f_s, f_pt = view(0), [view(1), view(2)], view(3).rearrange("p (b q) -> p b q", q=P)
        g_dec = view(0)
        g_kdec = view(1)
        g_att = view(2)
        g_u = view(3)
        g_nt, g_o = view(4), view(4)
        g_t = view(5)
        g_n = vT[:, :]
        state = [small[:, 0, :], small[:, 1, :]]
        ybuf = [small[:, 2, :], small[:, 3, :]]
        vnew = [small[:, 4, :], small[:, 5, :]]
        acc_gate = scr[:, 0:D]
        ada_gate = [scr[:, D:2 * D], scr[:, 2 * D:3 * D]]

        consts = sem("consts")
        gates_zeroed = sem("gates_zeroed")
        gates_w_put = sem("gates_w_put")
        cols_turned = sem("cols_turned")
        cols_ready = sem("cols_ready")
        lower_rows = sem("lower_rows")
        consts_done = sem("consts_done")
        small_in = sem("small_in")
        gates_w_in = sem("gates_w_in")
        silu_c = sem("silu_c")
        x_sq = sem("x_sq")
        x_ln = sem("x_ln")
        x_rstd = sem("x_rstd")
        x_scaled = sem("x_scaled")
        x_turned = sem("x_turned")
        x_kept = sem("x_kept")
        ada_added = sem("ada_added")
        mod_summed = sem("mod_summed")
        mod_biased = sem("mod_biased")
        mod_cols = sem("mod_cols")
        h_affine = sem("h_affine")
        h_hi_done = sem("h_hi_done")
        h_lo_even = sem("h_lo_even")
        h_lo_odd = sem("h_lo_odd")
        w_zeroed = sem("w_zeroed")
        w_hi = sem("w_hi")
        w_lo = sem("w_lo")
        w_used = sem("w_used")
        gates_dve = sem("gates_dve")
        gates_act = sem("gates_act")
        gates_turned = sem("gates_turned")
        gates_cols = sem("gates_cols")
        rows_stored = sem("rows_stored")
        gate_biased = sem("gate_biased")
        gate_added = sem("gate_added")
        gate_summed = sem("gate_summed")
        gate_row = sem("gate_row")
        gate_stored = sem("gate_stored")
        fox_taken = sem("fox_taken")
        fox_sq = sem("fox_sq")
        fox_ss = sem("fox_ss")
        fox_ln = sem("fox_ln")
        fox_rstd = sem("fox_rstd")
        fox_qk = sem("fox_qk")
        fox_vturn = sem("fox_vturn")
        fox_v = sem("fox_v")
        fox_bias_in = sem("fox_bias_in")
        fox_masked = sem("fox_masked")
        fox_scores = sem("fox_scores")
        fox_max = sem("fox_max")
        fox_exp = sem("fox_exp")
        fox_recip = sem("fox_recip")
        fox_probs = sem("fox_probs")
        fox_pturn = sem("fox_pturn")
        fox_pt = sem("fox_pt")
        fox_pv = sem("fox_pv")
        fox_half = sem("fox_half")
        fox_stored = sem("fox_stored")
        gdn_stored = sem("gdn_stored")
        head_conv = sem("head_conv")
        conv_first = sem("conv_first")
        conv_tap = sem("conv_tap")
        conv_silu = sem("conv_silu")
        dec_in = sem("dec_in")
        gdn_z = sem("gdn_z")
        gdn_cols = sem("gdn_cols")
        gdn_cexp = sem("gdn_cexp")
        gdn_sq = sem("gdn_sq")
        gdn_ss = sem("gdn_ss")
        gdn_ln = sem("gdn_ln")
        gdn_rstd = sem("gdn_rstd")
        gdn_qk = sem("gdn_qk")
        gdn_vturn = sem("gdn_vturn")
        gdn_v = sem("gdn_v")
        gdn_kturn = sem("gdn_kturn")
        gdn_kdec = sem("gdn_kdec")
        gdn_args = sem("gdn_args")
        gdn_decays = sem("gdn_decays")
        gdn_gram = sem("gdn_gram")
        gdn_att_mm = sem("gdn_att_mm")
        gdn_n = sem("gdn_n")
        gdn_att = sem("gdn_att")
        gdn_qe = sem("gdn_qe")
        gdn_nturn = sem("gdn_nturn")
        gdn_nt = sem("gdn_nt")
        gdn_t0 = sem("gdn_t0")
        gdn_t1 = sem("gdn_t1")
        gdn_uturn = sem("gdn_uturn")
        gdn_u1 = sem("gdn_u1")
        inv_p = sem("inv_p")
        inv_p_out = sem("inv_p_out")
        inv_t = sem("inv_t")
        inv_t_out = sem("inv_t_out")
        inv_u = sem("inv_u")
        inv_u_out = sem("inv_u_out")
        scan_z = sem("scan_z")
        scan_y = sem("scan_y")
        scan_v = sem("scan_v")
        scan_vnew = sem("scan_vnew")
        scan_upd = sem("scan_upd")
        scan_state = sem("scan_state")
        scan_o = sem("scan_o")
        scan_o_out = sem("scan_o_out")
        out_sq = sem("out_sq")
        out_ss = sem("out_ss")
        out_ln = sem("out_ln")
        out_rstd = sem("out_rstd")
        out_norm = sem("out_norm")
        gdn_done = sem("gdn_done")
        wo_hi_done = sem("wo_hi_done")
        wo_lo_done = sem("wo_lo_done")
        wo_used = sem("wo_used")
        gate_in = sem("gate_in")
        final_g_in = sem("final_g_in")
        m_hi_done = sem("m_hi_done")
        m_lo_done = sem("m_lo_done")
        x_again = sem("x_again")
        y_ready = sem("y_ready")
        y_gated = sem("y_gated")
        y_added = sem("y_added")
        y_sq = sem("y_sq")
        y_sum = sem("y_sum")
        y_ln = sem("y_ln")
        y_rstd = sem("y_rstd")
        y_done = sem("y_done")
        y_stored = sem("y_stored")
        x_loaded = [sem(f"x_loaded{i}") for i in range(4)]
        ada_loaded = [sem(f"ada_loaded{i}") for i in range(6)]
        w_loaded = [sem(f"w_loaded{i}") for i in range(4)]
        staged = [gq[:, :], gk[:, :], gz[:, :], flatb(gv)]
        gate_loaded = [sem("gate_loaded0"), sem("gate_loaded1")]
        m_loaded = [sem(f"m_loaded{i}") for i in range(4)]
        wo_loaded = [sem(f"wo_loaded{i}") for i in range(4)]

        def blocks(ap, n=NB):
            return ap.rearrange("p (b q) -> p b q", b=n)

        def blk(ap, j):
            return ap[:, j * P:(j + 1) * P]

        def half(ap, g):
            return ap[:, g * HALF:(g + 1) * HALF]

        def spread(col, n):
            return col.unsqueeze(2).to_broadcast([P, n, P])

        def over_blocks(mat, n):
            return mat.unsqueeze(1).to_broadcast([P, n, P])

        def side(mat, lv, which):
            return mat.rearrange("p (b u s) -> p b u s", u=2, s=1 << lv)[:, :, which, :]

        def sides(mats, lv, which):
            return mats.rearrange("p (j b u s) -> p j b u s", j=4, u=2, s=1 << lv)[:, :, :, which, :]

        def half_blk(bank, j):
            return bank[:, j * (P // 2):(j + 1) * (P // 2)]

        def compact(bank, lv):
            return bank[:, 0:HALF // 2].rearrange("p (j b s) -> p j b s", j=4, s=1 << lv)

        GATES_ROWS = 2 + 8 + 1 + NB + 2

        def scale_x(dve, t):
            dve.wait_ge(x_rstd, t + 1)
            dve.tensor_scalar(x_in[:, t % 4, :], x_in[:, t % 4, :], xstat[:, 16 + t:17 + t], None, ALU.mult)\
                .then_inc(x_scaled, 1)

        def keep(act, t):
            for g in range(4):
                act.wait_ge(x_turned, 4 * t + g + 1)
                act.activation(xT[:, 4 * g:4 * g + 4, t * P:(t + 1) * P],
                               (mA, mB, mC, mD)[g].rearrange("p (i q) -> p i q", q=P), ACT.Copy)\
                    .then_inc(x_kept, 1)

        def is_zero(m):
            return isinstance(m, int) and m == 0

        D0, A0, B0 = 1, 5, 9

        def n_groups(n):
            return 2 if NB - n > 4 else 1

        def groups_before(n):
            return 2 * n if n < 4 else 8 + (n - 4)

        GROUPS = groups_before(NB)

        def fox_slot(n, gap):
            return 7 + gap * n

        GAP, LAST_GAP = 7, 4
        LAST_SLOTS = fox_slot(NB, LAST_GAP) + 3
        ORDER = [2 * H - 1] + [i for i in range(2 * H - 1) if i != H - 1] + [H - 1]

        def first_row(idx, t):
            return (4 * (1 - idx // 4) + t) * P

        INV0 = 16
        SCAN0 = INV0 + 2 * (LEVELS - 1) + 1

        def scan_slot(j):
            return SCAN0 + 4 * j

        def add_x(pool, idx, t):
            hf, ch = idx // 4, idx % 4
            pool.wait_ge(y_gated, 4 * idx + t + 1)
            if ch == 0:
                pool.wait_ge(x_again, 64 * hf + 64)
            dst = y[:, t, ch * HALF:(ch + 1) * HALF]
            pool.tensor_tensor(dst, dst, gated[:, t, :], ALU.add).then_inc(y_added, 1)

        block = ctx.enter_context(nc.Block())

        @block.sync
        def _(sp):
            def load_x(t):
                if t >= 4:
                    sp.wait_ge(x_turned, 4 * (t - 3))
                sp.dma_start(x_in[:, t % 4, :], xs[t * P:(t + 1) * P, :]).then_inc(x_loaded[t % 4], 16)

            def load_ada(n):
                kt, part = n // 2, n % 2
                if n >= 6:
                    sp.wait_ge(ada_added, n - 5)
                sp.dma_start(ada[:, n % 6, :], w_ada_v[:, kt, part * D:(part + 1) * D])\
                    .then_inc(ada_loaded[n % 6], 16)

            load_x(0)
            for n in range(2 * KT):
                load_ada(n)
                if n % 3 == 0 and n // 3 + 1 < NB:
                    load_x(n // 3 + 1)

            def load_w(b, p, src, col):
                sp.wait_ge(w_lo, 4 * b + p - 3)
                sp.dma_start(w_raw[:, p, :, :], src[:, 4 * p:4 * p + 4, col]).then_inc(w_loaded[p], 16)

            for n in range(4):
                for p in range(4):
                    load_w(1 + n, p, w_in_v, slice(GDN_COL[n], GDN_COL[n] + P))
                    i = 4 * n + p
                    for kt in {7: (0,), 8: (1,), 9: (2,), 10: (3,), 11: (4, 5), 12: (6, 7), 13: (8, 9),
                               14: (10, 11), 15: (12, 13, 14, 15)}.get(i, ()):
                        if kt >= 2:
                            sp.wait_ge(gate_added, kt - 1)
                        sp.dma_start(ada_gate[kt % 2], w_ada_v[:, kt, 2 * D:3 * D])\
                            .then_inc(gate_loaded[kt % 2], 16)
                    if n == 2 and p == 3:
                        sp.wait_ge(gates_dve, GATES_ROWS)
                        sp.dma_start(rows_dram[1], fq[0:H, :]).then_inc(rows_stored, 16)
                        sp.dma_start(rows_dram[0], fq[32:32 + H, :]).then_inc(rows_stored, 16)
            for p in range(4):
                load_w(A0, p, w_in_v, slice(FOX_COL[0], FOX_COL[0] + P))
            sp.wait_ge(gate_added, KT)
            sp.dma_start(ada_gate[0][0:1, :], b_ada[:, 2 * D:3 * D]).then_inc(gate_biased, 16)
            sp.wait_ge(gate_row, 1)
            sp.dma_start(gate_dram, ada_gate[1][0:1, :]).then_inc(gate_stored, 16)

            def part_A(m, col, last_fox):
                for n in range(4):
                    for p in range(4):
                        if n or not is_zero(m):
                            load_w(8 * m + A0 + n, p, w_in_v, bass.ds(col + FOX_COL[n], P))
                    if n == 0:
                        if not is_zero(m):
                            sp.wait_ge(fox_half, 2 * m)
                        sp.dma_start(g_dec, rows_dram[0, bass.ds(m, 1), :].to_broadcast([P, SEQ]))\
                            .then_inc(dec_in, 16)
                        if not is_zero(m):
                            sp.dma_start(mixed_dram[bass.ds(last_fox, 1)].rearrange("o p t -> (o p) t"), fz[:, :])\
                                .then_inc(fox_stored, 16)

            def bias_in(m, this_gdn):
                sp.wait_ge(gdn_done, m + 1)
                sp.dma_start(f_bias, rows_dram_flat[bass.ds(this_gdn, 1), :].to_broadcast([P, SEQ]))\
                    .then_inc(fox_bias_in, 16)

            def part_B(m, col, this_gdn):
                for n in range(4):
                    for p in range(4):
                        load_w(8 * m + B0 + n, p, w_in_v, bass.ds(col + GDN_COL[n] + P, P))
                    if n == 0:
                        bias_in(m, this_gdn)
                        sp.dma_start(mixed_dram[bass.ds(this_gdn, 1)].rearrange("o p t -> (o p) t"), g_o)\
                            .then_inc(gdn_stored, 16)

            sp.wait_ge(rows_stored, 32)
            sp.wait_ge(gate_stored, 16)
            part_A(0, 0, None)
            part_B(0, 0, H)
            with sp.Fori(1, H - 1) as m:
                col = sp.snap(m * P)
                last_fox, this_gdn = sp.snap(m - 1), sp.snap(m + H)
                part_A(m, col, last_fox)
                part_B(m, col, this_gdn)
            part_A(H - 1, (H - 1) * P, H - 2)

            def load_wo(q):
                k, cols = q % KT, slice(q // KT % 4 * HALF, (q // KT % 4 + 1) * HALF)
                if q >= 4:
                    sp.wait_ge(wo_lo_done, q - 3)
                else:
                    sp.wait_ge(w_lo, 4 * (8 * H + 1) + q - 3)
                sp.dma_start(wo_raw[:, k % 4, :], w_out_v[:, ORDER[k], cols]).then_inc(wo_loaded[k % 4], 16)

            for k in range(4):
                load_wo(k)
            bias_in(H - 1, 2 * H - 1)
            sp.wait_ge(fox_stored, 16 * (H - 1))
            sp.wait_ge(gdn_stored, 16 * (H - 1))
            for k in range(1, KT - 1):
                if k > 4:
                    sp.wait_ge(m_lo_done, k - 3)
                sp.dma_start(staged[k % 4], mixed_dram[ORDER[k]]).then_inc(m_loaded[k % 4], 16)
                load_wo(k + 3)
            load_wo(KT + 2)

            def load_x_again(hf, t):
                if hf:
                    sp.wait_ge(y_stored, 16 * 4)
                sp.dma_start(y[:, t, :], xs[first_row(4 * hf, t):first_row(4 * hf, t) + P, :]).then_inc(x_again, 16)

            def store_y(hf, t):
                sp.wait_ge(y_done, 4 * hf + t + 1)
                sp.dma_start(outs[first_row(4 * hf, t):first_row(4 * hf, t) + P, :], y[:, t, :])\
                    .then_inc(y_stored, 16)

            sp.wait_ge(m_lo_done, KT + 1)
            for idx in range(1, 8):
                for k in range(KT):
                    q = idx * KT + k
                    if q >= KT + 3:
                        load_wo(q)
                    if idx == 1 and k == 2:
                        sp.dma_start(gate_all[:, :], gate_dram.to_broadcast([P, D])).then_inc(gate_in, 16)
                    if idx == 1 and k in (4, 6, 8, 10):
                        load_x_again(0, (k - 4) // 2)
                    if idx == 1 and k == 12:
                        sp.dma_start(fg_all[:, :], final_g.rearrange("(a n) -> a n", a=1).to_broadcast([P, D]))\
                            .then_inc(final_g_in, 16)
                    if idx == 4 and k == KT - 2:
                        store_y(0, 0)
                    if idx == 5 and k in (0, 2, 4):
                        store_y(0, k // 2 + 1)
                    if idx == 5 and 6 <= k < 10:
                        load_x_again(1, k - 6)
            for t in range(4):
                store_y(1, t)
            sp.wait_ge(y_stored, 16 * NB)

        @block.gpsimd
        def _(pool):
            pool.memset(w_raw[:, :, :, :], 0.0).then_inc(w_zeroed, 1)
            pool.memset(gatecol[:, :], 0.0).then_inc(gates_zeroed, 1)
            pool.wait_ge(gates_zeroed, 1)
            pool.memset(gatecol[0:32, 0:1], -1.0).then_inc(gates_zeroed, 1)
            pool.wait_ge(gates_zeroed, 2)
            pool.memset(gatecol[32:64, 0:1], 1.0).then_inc(gates_zeroed, 1)
            pool.wait_ge(gates_zeroed, 3)
            n = 0
            for t, v in ((ident, 0.0), (ones, 1.0), (causal_fox, 0.0), (causal_t, 0.0), (strict, 0.0),
                         (level, 1.0)):
                pool.memset(t[tuple([slice(None)] * len(t.shape))], v).then_inc(consts, 1)
                n += 1
            pool.memset(eps[:, :], EPS).then_inc(consts, 1)
            n += 1
            pool.wait_ge(consts, n)
            for t, op, fill, step in ((ident, ALU.not_equal, 1.0, (-1, 1)), (causal_fox, ALU.is_ge, -BIG, (-1, 1)),
                                      (causal_t, ALU.is_ge, -BIG, (1, -1)), (strict, ALU.is_gt, BIG, (-1, 1))):
                pool.affine_select(out=t[:, :], in_=t[:, :], compare_op=op, fill=fill, base=0,
                                   pattern=[[step[0], P]], channel_multiplier=step[1]).then_inc(consts, 1)
                n += 1
            for lv in range(LEVELS):
                size = 1 << lv
                cols = P // (2 * size)
                v = level[:, lv, :].rearrange("p (b u s) -> p b u s", u=2, s=size)
                for base, pat, cm in ((-size, [[-2 * size, cols], [0, 2], [0, size]], 1),
                                      (2 * size - 1, [[2 * size, cols], [0, 2], [0, size]], -1),
                                      (0, [[0, cols], [-1, 2], [0, size]], 0)):
                    pool.wait_ge(consts, n)
                    pool.affine_select(out=v, in_=v, compare_op=ALU.is_ge, fill=0.0, base=base,
                                       pattern=pat, channel_multiplier=cm).then_inc(consts, 1)
                    n += 1
            pool.wait_ge(gates_w_in, 32)
            pool.tensor_copy(w_raw[:, :, :, 64:64 + H], w_raw[:, :, :, 32 + H:32 + 2 * H]).then_inc(gates_w_put, 1)
            pool.memset(dummy[:, :], 0.0).then_inc(consts_done, 1)

            def split_lo(b, p):
                pool.wait_ge(w_hi, 4 * b + p + 1)
                pool.tensor_tensor(wr_lo[:, p, :, :], w_raw[:, p, :, :], wr_hi[:, p, :, :].bitcast(F32),
                                   ALU.subtract).then_inc(w_lo, 1)

            for p in range(4):
                split_lo(0, p)
            for kt in range(1, KT, 2):
                pool.wait_ge(h_hi_done, kt + 1)
                pool.tensor_tensor(h_lo[:, kt, :], xT[:, kt, :], h_hi[:, kt, :].bitcast(F32), ALU.subtract)\
                    .then_inc(h_lo_odd, 1)

            def split_wo(q):
                pool.wait_ge(wo_hi_done, q + 1)
                pool.tensor_tensor(wo_lo[:, q % 4, :], wo_raw[:, q % 4, :], wo_hi[:, q % 4, :].bitcast(F32),
                                   ALU.subtract).then_inc(wo_lo_done, 1)

            def split_ahead(b0, slot, last=False):
                if slot % 4 == 0:
                    at = slot // 4 + 2
                    if last and at >= 16:
                        split_wo(at - 16)
                    else:
                        split_lo(b0 + at // 4, at % 4)

            split_lo(1, 0)
            split_lo(1, 1)
            for slot in range(SLOTS):
                split_ahead(1, slot)

            def fox_mask(m, n):
                if n == 0:
                    pool.wait_ge(fox_bias_in, 16 * m + 16)
                else:
                    pool.wait_ge(fox_max, 8 * m + n)
                b = blk(f_bias, NB - 1 - n)
                pool.tensor_tensor(b, b, causal_fox[:, :], ALU.add).then_inc(fox_masked, 1)

            def part_B(m):
                for slot in range(SLOTS):
                    split_ahead(8 * m + B0, slot)
                    for n in range(NB):
                        if slot == fox_slot(n, GAP) - 4:
                            fox_mask(m, n)

            def gdn(m, slot):
                if slot == 11:
                    pool.wait_ge(gdn_att_mm, 2 * m + 2)
                    pool.wait_ge(gdn_decays, 3 * m + 3)
                    pool.tensor_tensor(gq[:, :], gq[:, :], g_dec, ALU.mult).then_inc(gdn_qe, 1)

            def part_A(m, last=False):
                for slot in range(SLOTS):
                    split_ahead(8 * m + A0, slot, last)
                    gdn(m, slot)

            part_A(0)
            part_B(0)
            with pool.Fori(1, H - 1) as m:
                part_A(m)
                part_B(m)
            part_A(H - 1, last=True)

            for slot in range(LAST_SLOTS):
                for n in range(NB):
                    if slot == fox_slot(n, LAST_GAP) - 4:
                        fox_mask(H - 1, n)
                k = (slot - 2) // 2
                if slot >= 2 and slot % 2 == 0 and 2 <= k < KT + 2:
                    split_wo(k)

            for idx in range(1, 8):
                for k in range(KT):
                    q = idx * KT + k + 2
                    if q < 8 * KT:
                        split_wo(q)
                    if k in (8, 10, 12, 14):
                        add_x(pool, idx - 1, (k - 8) // 2)
            for t in range(4):
                add_x(pool, 7, t)

        @block.tensor
        def _(pe):
            pe.wait_ge(consts_done, 1)
            banks = (mA, mB, mC, mD)
            pe.wait_ge(small_in, 16 * 10)
            pe.transpose(pair[1][:, 0:5 * KT + 3], rows_in[0:5 * KT + 3, 0, :], ident[0:5 * KT + 3, 0:5 * KT + 3])
            pe.transpose(pair[1][:, P:P + 3 * H * TAPS], rows_in[0:3 * H * TAPS, 1, :],
                         ident[0:3 * H * TAPS, 0:3 * H * TAPS]).then_inc(cols_turned, 1)
            for t in range(NB):
                pe.wait_ge(x_scaled, t + 1)
                for g in range(4):
                    if t:
                        pe.wait_ge(x_kept, 4 * (t - 1) + g + 1)
                    for i in range(4):
                        mm = pe.transpose(blk(banks[g], i), blk(x_in[:, t % 4, :], 4 * g + i), ident[:, :])
                    mm.then_inc(x_turned, 1)
            pe.wait_ge(ada_added, 2 * KT)
            for n in range(2 * KT):
                mm = pe.matmul(pair[0][:, n:n + 1], blk(acc[:, n // KT, :], n % KT), ones[:, 0:1],
                               start=True, stop=True)
            mm.then_inc(mod_summed, 1)

            def pair_taken(m, k0, n):
                if k0 == B0 and n < 2:
                    pe.wait_ge(fox_taken, 4 * m + 3 + n)
                elif k0 == B0:
                    pe.wait_ge(conv_tap, 9 * m + 9 + 3 * (n - 2) + 3)
                elif k0 == A0 and n == 0:
                    pe.wait_ge(conv_tap, 9 * m + 9)
                elif k0 == A0 and n == 1:
                    pe.wait_ge(gdn_z, m + 1)
                elif k0 == A0:
                    pe.wait_ge(fox_taken, 4 * m + n - 1)
                elif k0 == D0 and n == 1:
                    pe.wait_ge(gates_act, 2)
                elif k0 == D0 and n >= 2:
                    pe.wait_ge(conv_tap, 3 * (n - 2) + 3)

            def project(m, k0, slot):
                n, kt = slot // KT, slot % KT
                p = kt // 4
                b = 8 * m + k0 + n
                to = pair[(k0 + n) % 2]
                if kt % 4 == 0:
                    pe.wait_ge(w_lo, 4 * b + p + 1)
                if kt == 0:
                    pair_taken(m, k0, n)
                if k0 == 0:
                    pe.wait_ge(h_lo_odd if kt % 2 else h_lo_even, kt // 2 + 1)
                hi, lo = wr_hi[:, p, kt % 4, :], wr_lo[:, p, kt % 4, :]
                for i, (w, h) in enumerate(((hi, h_hi), (hi, h_lo), (lo, h_hi))):
                    for g in range(2):
                        mm = pe.matmul(half(to, g), w, half(h[:, kt, :], g), start=(kt == 0 and i == 0),
                                       stop=(kt == KT - 1 and i == 2))
                if kt % 4 == 3:
                    mm.then_inc(w_used, 1)

            def column_sums(to, sq):
                for g in range(2):
                    mm = pe.matmul(to[g], ones[:, :], half(sq, g), start=True, stop=True)
                return mm

            def fox(m, slot, gap=GAP):
                if slot == 2:
                    pe.wait_ge(fox_sq, 2 * m + 1)
                    column_sums((mA, mB), f_s[0]).then_inc(fox_ss, 1)
                if slot == 3:
                    pe.wait_ge(fox_sq, 2 * m + 2)
                    column_sums((mC, mD), f_s[1]).then_inc(fox_ss, 1)
                if slot == 6:
                    pe.wait_ge(fox_taken, 4 * m + 4)
                    pe.wait_ge(fox_ln, 2 * m + 2)
                    for g in range(2):
                        for j in range(4):
                            mm = pe.transpose(blk((mC, mD)[g], j), blk(vT[:, :], 4 * g + j), ident[:, :])
                        mm.then_inc(fox_vturn, 1)
                for n in range(NB):
                    i = NB - 1 - n
                    at = fox_slot(n, gap)
                    if slot == at:
                        if n == 0:
                            pe.wait_ge(fox_ln, 2 * m + 2)
                            pe.wait_ge(fox_qk, 2 * m + 2)
                        else:
                            pe.wait_ge(fox_max, 8 * m + n)
                        for g in range(n_groups(n)):
                            keys = slice(g * HALF, min((g + 1) * HALF, (i + 1) * P))
                            mm = pe.matmul(mAB[:, keys], blk(fq[:, :], i), fk[:, keys], start=True, stop=True)
                        mm.then_inc(fox_scores, 1)
                    for g in range(n_groups(n)):
                        if slot == at + 4 + g:
                            if g == 0:
                                pe.wait_ge(fox_probs, 8 * m + n + 1)
                            if n == 0 and g == 0:
                                pe.wait_ge(fox_v, 2 * m + 2)
                            else:
                                pe.wait_ge(fox_pt, GROUPS * m + groups_before(n) + g)
                            for j in range(4 * g, min(4 * g + 4, i + 1)):
                                mm = pe.transpose(blk(mC, j % 4), blk(f_s[n % 2], j), ident[:, :])
                            mm.then_inc(fox_pturn, 1)
                    if slot == at + 6:
                        pe.wait_ge(fox_pt, GROUPS * m + groups_before(n + 1))
                        if n == 4:
                            pe.wait_ge(fox_half, 2 * m + 1)
                        for j in range(i + 1):
                            mm = pe.matmul(blk(mD, i % 4), fv[:, j, :], f_pt[:, j, :],
                                           start=(j == 0), stop=(j == i))
                        mm.then_inc(fox_pv, 1)

            def gdn(m, slot):
                if slot == 2:
                    pe.wait_ge(gdn_sq, 2 * m + 1)
                    column_sums((mA, mB), view(1)).then_inc(gdn_ss, 1)
                    pe.wait_ge(gdn_sq, 2 * m + 2)
                    column_sums((mC, mD), view(3)).then_inc(gdn_ss, 1)
                if slot == 6:
                    pe.wait_ge(gdn_ln, 2 * m + 1)
                    pe.wait_ge(conv_silu, 3 * m + 1)
                    for g in range(2):
                        for j in range(4):
                            mm = pe.transpose(blk((mA, mB)[g], j), blk(vT[:, :], 4 * g + j), ident[:, :])
                        mm.then_inc(gdn_vturn, 1)
                if slot == 7:
                    pe.wait_ge(gdn_ln, 2 * m + 2)
                    pe.wait_ge(gdn_qk, 2 * m + 2)
                    for g in range(2):
                        for j in range(4):
                            mm = pe.transpose(blk((mC, mD)[g], j), blk(gk[:, :], 4 * g + j), ident[:, :])
                        mm.then_inc(gdn_kturn, 1)
                if slot == 9:
                    pe.wait_ge(gdn_v, 2 * m + 2)
                    for g in range(2):
                        for j in range(4):
                            kb = blk(gk[:, :], 4 * g + j)
                            mm = pe.matmul(blk((mA, mB)[g], j), kb, kb, start=True, stop=True)
                        mm.then_inc(gdn_gram, 1)
                if slot == 10:
                    pe.wait_ge(gdn_kdec, 2 * m + 2)
                    for g in range(2):
                        for j in range(4):
                            mm = pe.matmul(blk((mC, mD)[g], j), blk(gk[:, :], 4 * g + j),
                                           blk(gq[:, :], 4 * g + j), start=True, stop=True)
                        mm.then_inc(gdn_att_mm, 1)
                if slot == 12:
                    pe.wait_ge(gdn_n, 8 * m + 8)
                    for g in range(2):
                        for j in range(4):
                            mm = pe.transpose(blk((mA, mB)[g], j), blk(g_n, 4 * g + j), ident[:, :])
                        mm.then_inc(gdn_nturn, 1)
                if slot == 15:
                    pe.wait_ge(gdn_t1, 2 * m + 2)
                    pe.wait_ge(gdn_att, 2 * m + 2)
                    for g in range(2):
                        for j in range(4):
                            mm = pe.transpose(blk((mC, mD)[g], j), blk(g_t, 4 * g + j), ident[:, :])
                        mm.then_inc(gdn_uturn, 1)
                L = LEVELS - 1
                for lv in range(1, LEVELS):
                    i = lv - 1
                    if slot == INV0 + 2 * i:
                        if i == 0:
                            pe.wait_ge(gdn_nt, 2 * m + 2)
                            pe.wait_ge(gdn_u1, 2 * m + 2)
                        else:
                            pe.wait_ge(inv_t_out, 2 * (L - 1) * m + 2 * i)
                            pe.wait_ge(inv_u_out, 2 * L * m + 2 * i)
                        for g in range(2):
                            for j in range(4):
                                mm = pe.matmul(half_blk((mA, mB)[g], j), blk(g_nt, 4 * g + j),
                                               side(blk(g_t, 4 * g + j), lv, 0), start=True, stop=True)
                            mm.then_inc(inv_p, 1)
                    if slot == INV0 + 2 * i + 1:
                        for g in range(2):
                            pe.wait_ge(inv_p_out, 2 * L * m + 2 * i + g + 1)
                            if lv < LEVELS - 1:
                                for j in range(4 * g, 4 * g + 4):
                                    mm = pe.matmul(half_blk((mC, mD)[g], j % 4), blk(g_u, j),
                                                   side(blk(g_n, j), lv, 0), start=True, stop=True)
                                mm.then_inc(inv_t, 1)
                            for j in range(4 * g, 4 * g + 4):
                                mm = pe.matmul(half_blk((mA, mB)[g], j % 4), blk(g_n, j),
                                               side(blk(g_u, j), lv, 1), start=True, stop=True)
                            mm.then_inc(inv_u, 1)
                for j in range(NB):
                    at = scan_slot(j)
                    if slot == at and j > 0:
                        pe.wait_ge(scan_state, 7 * m + j)
                        if j == 1:
                            pe.wait_ge(inv_u_out, 2 * L * m + 2 * L)
                        pe.matmul(mA[:, 0:P], blk(gk[:, :], j), state[j % 2], start=True, stop=True)\
                            .then_inc(scan_z, 1)
                    if slot == at + 1:
                        if j == 0:
                            pe.wait_ge(inv_u_out, 2 * L * m + 2 * L)
                            y_in = gv[:, 0, :]
                        else:
                            pe.wait_ge(scan_y, 7 * m + j)
                            y_in = ybuf[j % 2]
                        pe.matmul(mB[:, 0:P], blk(g_u, j), y_in, start=True, stop=True).then_inc(scan_v, 1)
                    if slot == at + 2:
                        pe.wait_ge(scan_vnew, 8 * m + j + 1)
                        if j < NB - 1:
                            pe.matmul(mC[:, 0:P], blk(g_kdec, j), vnew[j % 2], start=True, stop=True)\
                                .then_inc(scan_upd, 1)
                        if j == 0:
                            pe.wait_ge(gdn_qe, m + 1)
                        if j == 4:
                            pe.wait_ge(scan_o_out, 2 * m + 1)
                        if j > 0:
                            pe.matmul(blk(mD, j % 4), state[j % 2], blk(gq[:, :], j), start=True, stop=False)
                        pe.matmul(blk(mD, j % 4), vnew[j % 2], blk(g_att, j), start=(j == 0), stop=True)\
                            .then_inc(scan_o, 1)
                if slot == SLOTS - 3:
                    pe.wait_ge(out_sq, 2 * m + 2)
                    column_sums((mA, mB), g_t).then_inc(out_ss, 1)

            pe.wait_ge(mod_cols, 1)
            for slot in range(KT):
                project(0, 0, slot)
            for slot in range(SLOTS):
                project(0, D0, slot)
                if slot == 48:
                    pe.wait_ge(gates_dve, GATES_ROWS)
                    for j in range(NB):
                        mm = pe.transpose(blk(mAB, j)[:, 0:96], blk(fq[0:96, :], j), ident[0:96, 0:96])
                    mm.then_inc(gates_turned, 1)
            pe.wait_ge(gates_cols, 2)
            pe.wait_ge(gate_added, KT)
            for g in range(4):
                mm = pe.matmul(ps[0:1, 4 + g, :], ones[:, 0:1], acc_gate[:, g * HALF:(g + 1) * HALF],
                               start=True, stop=True)
            mm.then_inc(gate_summed, 1)

            def part_B(m):
                for slot in range(SLOTS):
                    project(m, B0, slot)
                    fox(m, slot)

            def part_A(m):
                for slot in range(SLOTS):
                    project(m, A0, slot)
                    gdn(m, slot)

            def y_tile(idx, k):
                q = idx * KT + k
                i = ORDER[k]
                pe.wait_ge(wo_lo_done, q + 1)
                if idx == 0:
                    pe.wait_ge(m_lo_done, k + 1)
                if idx == 4 and k == 0:
                    pe.wait_ge(m_lo_done, KT + 1)
                for t in range(4):
                    tok = slice(first_row(idx, t), first_row(idx, t) + P)
                    if k == 0 and idx >= 2:
                        pe.wait_ge(y_gated, 4 * (idx - 2) + t + 1)
                    to = ps[:, idx % 2 * 4 + t, :]
                    hi, lo = m_hi[:, i, tok], m_lo[:, i, tok]
                    for j, (a, w) in enumerate(((hi, wo_hi), (hi, wo_lo), (lo, wo_hi))):
                        mm = pe.matmul(to, a, w[:, k % 4, :], start=(k == 0 and j == 0),
                                       stop=(k == KT - 1 and j == 2))
                    if k == KT - 1:
                        mm.then_inc(y_ready, 1)
                    elif t == 3:
                        mm.then_inc(wo_used, 1)

            part_A(0)
            part_B(0)
            with pe.Fori(1, H - 1) as m:
                part_A(m)
                part_B(m)
            part_A(H - 1)

            pe.wait_ge(fox_taken, 4 * H)
            for slot in range(LAST_SLOTS):
                fox(H - 1, slot, LAST_GAP)
                if slot >= 4 and slot % 2 == 0 and (slot - 4) // 2 < KT:
                    y_tile(0, (slot - 4) // 2)
            pe.wait_ge(fox_half, 2 * H)
            for idx in range(1, 8):
                for k in range(KT):
                    y_tile(idx, k)

        @block.scalar
        def _(act):
            for row, vec in ((0, c), (KT, norm_g), (2 * KT, b_ada), (5 * KT, fox_qn_g), (5 * KT + 1, fox_kn_g),
                             (5 * KT + 2, gdn_norm_g)):
                n = vec.shape[1] // P
                act.dma_start(rows_in[row:row + n, 0, :], vec.rearrange("a (t p) -> (a t) p", p=P)).then_inc(small_in, 16)
            act.dma_start(rows_in[0:3 * H * TAPS, 1, :], gdn_conv_w[0].rearrange("k (t p) -> (k t) p", p=P))\
                .then_inc(small_in, 16)
            act.wait_ge(gates_zeroed, 3)
            act.dma_start(gatecol[0:H, 1:2], b_fgate.rearrange("a h -> h a")).then_inc(small_in, 16)
            act.dma_start(gatecol[32:32 + H, 1:2], gdn_dt_bias.rearrange("a h -> h a")).then_inc(small_in, 16)
            act.dma_start(gatecol[32:32 + H, 2:3], gdn_A_log.rearrange("a h -> h a")).then_inc(small_in, 16)
            act.wait_ge(w_zeroed, 1)
            for to, col, n in ((0, COL_F, H), (32, COL_AB, 2 * H)):
                act.dma_start(w_raw[:, :, :, to:to + n].rearrange("p a b n -> p (a b) n"),
                              w_in_v[:, :, col:col + n]).then_inc(gates_w_in, 16)
            act.wait_ge(cols_ready, 1)
            act.activation(c_col, c_col, ACT.Silu).then_inc(silu_c, 1)
            act.wait_ge(consts, 7)
            for t in range(NB):
                act.wait_ge(x_loaded[t % 4], 16 * (t // 4 + 1))
                act.activation(junk[:, :], x_in[:, t % 4, :], ACT.Square, accum_out=xstat[:, t:t + 1])\
                    .then_inc(x_sq, 1)
                act.wait_ge(x_sq, t + 1)
                act.activation(xstat[:, 8 + t:9 + t], xstat[:, t:t + 1], ACT.Ln, bias=eps[:, :], scale=1.0 / D)\
                    .then_inc(x_ln, 1)
                act.wait_ge(x_ln, t + 1)
                act.activation(xstat[:, 16 + t:17 + t], xstat[:, 8 + t:9 + t], ACT.Exp, scale=-0.5)\
                    .then_inc(x_rstd, 1)
                if t:
                    keep(act, t - 1)
            keep(act, NB - 1)
            def split_hi(b, p, col=None):
                if b is None:
                    act.wait_ge(gates_w_put, 1)
                else:
                    act.wait_ge(w_loaded[p], 16 * b)
                    act.wait_ge(w_used, 4 * b + p - 3)
                act.activation(wr_hi[:, p, :, :], w_raw[:, p, :, :], ACT.Copy).then_inc(w_hi, 1)

            def split_wo(q):
                act.wait_ge(wo_loaded[q % 4], 16 * (q // 4 + 1))
                if q < 4:
                    act.wait_ge(w_used, 4 * (8 * H + 1) + q - 3)
                elif (q - 4) % KT == KT - 1:
                    act.wait_ge(y_ready, 4 * ((q - 4) // KT) + 4)
                else:
                    act.wait_ge(wo_used, (KT - 1) * ((q - 4) // KT) + (q - 4) % KT + 1)
                act.activation(wo_hi[:, q % 4, :], wo_raw[:, q % 4, :], ACT.Copy).then_inc(wo_hi_done, 1)

            def split_ahead(b0, slot, last=False):
                if slot % 4 == 0:
                    at = slot // 4 + 2
                    if last and at >= 16:
                        split_wo(at - 16)
                    else:
                        split_hi(b0 + at // 4, at % 4)

            for p in range(4):
                split_hi(None, p)
            act.wait_ge(mod_cols, 1)
            act.wait_ge(x_kept, 4 * NB)
            for kt in range(KT):
                act.activation(xT[:, kt, :], xT[:, kt, :], ACT.Identity, bias=s_col[:, kt:kt + 1],
                               scale=a_col[:, kt:kt + 1]).then_inc(h_affine, 1)

            for p in range(4):
                split_hi(1, p)

            act.wait_ge(w_used, 4)
            act.wait_ge(gates_dve, 2)
            act.activation(fq[0:64, :], pair[0][0:64, :], ACT.Identity, bias=gatecol[0:64, 1:2],
                           scale=gatecol[0:64, 0:1]).then_inc(gates_act, 1)
            act.activation(fq[64:96, :], pair[0][64:96, :], ACT.Exp, scale=-1.0)\
                .then_inc(gates_act, 1)
            act.activation(gatecol[0:64, 2:3], gatecol[0:64, 2:3], ACT.Exp).then_inc(gates_act, 1)
            act.wait_ge(gates_act, 1)
            act.activation(fk[0:64, :], fq[0:64, :], ACT.Abs).then_inc(gates_act, 1)
            act.wait_ge(gates_act, 4)
            act.activation(fk[0:64, :], fk[0:64, :], ACT.Exp, scale=-1.0).then_inc(gates_act, 1)
            act.wait_ge(gates_dve, 3)
            act.activation(flatb(fv)[0:64, :], fz[0:64, :], ACT.Ln).then_inc(gates_act, 1)

            def take_fox(m, n):
                b, used = 8 * m + A0 + n, (A0 + n) % 2
                act.wait_ge(w_used, 4 * b + 4)
                if n == 0 and not is_zero(m):
                    act.wait_ge(fox_half, 2 * m)
                if n == 2 and not is_zero(m):
                    act.wait_ge(fox_stored, 16 * m)
                if n == 3:
                    act.wait_ge(inv_u, 2 * (LEVELS - 1) * m + 2 * (LEVELS - 1))
                to = (fq, fk, fz, vT)[n]
                act.activation(to[:, :], pair[used], ACT.Silu if n == 2 else ACT.Copy)\
                    .then_inc(fox_taken, 1)

            def take_gdn(m, n):
                b, used = 8 * m + D0 + n, (D0 + n) % 2
                act.wait_ge(w_used, 4 * b + 4)
                if n == 0:
                    if not is_zero(m):
                        act.wait_ge(fox_vturn, 2 * m)
                    act.wait_ge(head_conv, m + 1)
                if n == 3:
                    act.activation(gz[:, :], pair[used], ACT.Silu).then_inc(gdn_z, 1)
                else:
                    act.activation((vT, gq, gk)[n][:, :], pair[used], ACT.Copy,
                                   scale=hconv[:, CONV_AT[n], TAPS - 1:TAPS]).then_inc(conv_first, 1)

            def silu_gdn(m, n):
                act.wait_ge(conv_tap, 9 * m + 3 * n + 3)
                t = (vT, gq, gk)[n]
                act.activation(t[:, :], t[:, :], ACT.Silu).then_inc(conv_silu, 1)

            def fox(m, slot, gap=GAP):
                if slot == 0:
                    act.wait_ge(gdn_done, m + 1)
                    for i, t in enumerate((fq, fk)):
                        act.wait_ge(fox_taken, 4 * m + 2 + 2 * i)
                        act.activation(f_s[i], t[:, :], ACT.Square).then_inc(fox_sq, 1)
                if slot == 3:
                    for i, sums in enumerate((mAB, mCD)):
                        act.wait_ge(fox_ss, 2 * m + i + 1)
                        act.activation(f_s[i], sums, ACT.Ln, bias=eps[:, :], scale=1.0 / HD).then_inc(fox_ln, 1)
                    for i in range(2):
                        act.wait_ge(fox_ln, 2 * m + i + 1)
                        act.activation(f_s[i], f_s[i], ACT.Exp, scale=-0.5).then_inc(fox_rstd, 1)
                for n in range(NB):
                    if slot == fox_slot(n, gap) + 2:
                        s = f_s[n % 2][:, 0:(NB - n) * P]
                        act.wait_ge(fox_max, 8 * m + n + 1)
                        act.activation(s, s, ACT.Exp, bias=negmax[:, n:n + 1], scale=-1.0,
                                       accum_out=lsum[:, n:n + 1]).then_inc(fox_exp, 1)

            def gdn(m, slot):
                if slot == 0:
                    if not is_zero(m):
                        act.wait_ge(fox_half, 2 * m)
                    act.wait_ge(conv_silu, 3 * m + 3)
                    act.activation(view(1), gq[:, :], ACT.Square).then_inc(gdn_sq, 1)
                    act.activation(view(3), gk[:, :], ACT.Square).then_inc(gdn_sq, 1)
                if slot == 2:
                    rs = (view(1), view(3))
                    for i, sums in enumerate((mAB, mCD)):
                        act.wait_ge(gdn_ss, 2 * m + i + 1)
                        act.activation(rs[i], sums, ACT.Ln, bias=eps[:, :]).then_inc(gdn_ln, 1)
                    for i in range(2):
                        act.wait_ge(gdn_ln, 2 * m + i + 1)
                        act.activation(rs[i], rs[i], ACT.Exp, scale=-0.5).then_inc(gdn_rstd, 1)
                if slot == 4:
                    act.wait_ge(gdn_cols, 4 * m + 2)
                    act.activation(edl[:, :], edl[:, :], ACT.Exp).then_inc(gdn_cexp, 1)
                    act.activation(eg[:, :], hcol[:, 0:NB], ACT.Exp).then_inc(gdn_cexp, 1)
                if slot == 7:
                    act.wait_ge(gdn_args, 16 * m + 16)
                    act.activation(g_t, g_t, ACT.Exp, scale=-1.0).then_inc(gdn_decays, 1)
                    act.activation(g_att, g_att, ACT.Exp).then_inc(gdn_decays, 1)
                    act.activation(g_dec, g_dec, ACT.Exp).then_inc(gdn_decays, 1)
                if slot == 12:
                    if not is_zero(m):
                        act.wait_ge(gdn_stored, 16 * m)
                    for g in range(2):
                        act.wait_ge(gdn_nturn, 2 * m + g + 1)
                        act.activation(half(g_nt, g), (mA, mB)[g], ACT.Copy).then_inc(gdn_nt, 1)
                if slot == 15:
                    for g in range(2):
                        act.wait_ge(gdn_uturn, 2 * m + g + 1)
                        act.activation(half(g_u, g), (mC, mD)[g], ACT.Copy).then_inc(gdn_u1, 1)
                for j in range(NB):
                    if slot == scan_slot(j) + 1:
                        act.wait_ge(scan_v, 8 * m + j + 1)
                        act.activation(vnew[j % 2], mB[:, 0:P], ACT.Copy).then_inc(scan_vnew, 1)
                    if slot == scan_slot(j) + 2 and j in (3, 7):
                        act.wait_ge(scan_o, 8 * m + j + 1)
                        act.activation(half(g_o, j // 4), mD, ACT.Copy).then_inc(scan_o_out, 1)
                for g, at in enumerate((scan_slot(3) + 3, SLOTS - 4)):
                    if slot == at:
                        act.wait_ge(scan_o_out, 2 * m + g + 1)
                        act.activation(half(g_t, g), half(g_o, g), ACT.Square).then_inc(out_sq, 1)
                if slot == SLOTS - 3:
                    act.wait_ge(out_ss, m + 1)
                    act.activation(g_t, mAB, ACT.Ln, bias=eps[:, :], scale=1.0 / HD).then_inc(out_ln, 1)
                    act.wait_ge(out_ln, m + 1)
                    act.activation(g_t, g_t, ACT.Exp, scale=-0.5).then_inc(out_rstd, 1)

            def take_slots(m, slot):
                if slot in (16, 32, 48):
                    take_gdn(m, slot // KT - 1)
                if slot in (22, 38, 54):
                    silu_gdn(m, slot // KT - 1)

            for slot in range(SLOTS):
                if slot >= 8:
                    split_ahead(1, slot)
                take_slots(0, slot)
            take_gdn(0, 3)
            act.wait_ge(rows_stored, 32)
            act.wait_ge(gates_turned, 1)
            act.wait_ge(gate_stored, 16)

            def part_B(m):
                for slot in range(SLOTS):
                    split_ahead(8 * m + B0, slot)
                    fox(m, slot)
                    take_slots(m + 1, slot)
                take_gdn(m + 1, 3)

            def part_A(m, last=False):
                for slot in range(SLOTS):
                    split_ahead(8 * m + A0, slot, last)
                    gdn(m, slot)
                    if slot in (16, 32, 48):
                        take_fox(m, slot // KT - 1)
                take_fox(m, 3)

            part_A(0)
            part_B(0)
            with act.Fori(1, H - 1) as m:
                part_A(m)
                part_B(m)
            part_A(H - 1, last=True)

            def split_m(i, src, cols=slice(0, SEQ)):
                act.activation(m_hi[:, i, cols], src, ACT.Copy).then_inc(m_hi_done, 1)

            act.wait_ge(w_used, 4 * (8 * H + 1))
            act.wait_ge(gdn_done, H)
            split_m(ORDER[0], g_o)
            for slot in range(LAST_SLOTS):
                fox(H - 1, slot, LAST_GAP)
                k = (slot - 2) // 2
                if slot >= 2 and slot % 2 == 0 and k < KT + 2:
                    if k >= 2:
                        split_wo(k)
                    if 0 < k < KT - 1:
                        act.wait_ge(m_loaded[k % 4], 16 * ((k - 1) // 4 + 1))
                        split_m(ORDER[k], staged[k % 4])
                    elif k == KT - 1:
                        act.wait_ge(fox_half, 2 * H - 1)
                        split_m(H - 1, half(fz[:, :], 1), slice(HALF, SEQ))
            act.wait_ge(fox_half, 2 * H)
            split_m(H - 1, half(fz[:, :], 0), slice(0, HALF))

            def finish(idx, t):
                hf, ch = idx // 4, idx % 4
                act.wait_ge(y_added, 4 * idx + t + 1)
                done = 4 * idx + t
                if done >= 2:
                    act.wait_ge(y_sq, done - 1)
                act.activation(sq_out[:, done % 2, :], y[:, t, ch * HALF:(ch + 1) * HALF], ACT.Square,
                               accum_out=xstat[:, 4 * t + ch:4 * t + ch + 1]).then_inc(y_sq, 1)
                if ch == 3:
                    k = 4 * hf + t
                    act.wait_ge(y_sum, k + 1)
                    act.activation(xstat[:, 20 + t:21 + t], xstat[:, 16 + t:17 + t], ACT.Ln, bias=eps[:, :],
                                   scale=1.0 / D).then_inc(y_ln, 1)
                    act.wait_ge(y_ln, k + 1)
                    act.activation(xstat[:, 24 + t:25 + t], xstat[:, 20 + t:21 + t], ACT.Exp, scale=-0.5)\
                        .then_inc(y_rstd, 1)

            for idx in range(1, 8):
                for k in range(KT):
                    q = idx * KT + k + 2
                    if q < 8 * KT:
                        split_wo(q)
                    if k in (9, 11, 13, 15):
                        finish(idx - 1, (k - 9) // 2)
            for t in range(4):
                finish(7, t)

        @block.vector
        def _(dve):
            dve.wait_ge(cols_turned, 1)
            dve.tensor_copy(cols[:, :], pair[1][:, 0:5 * KT + 3]).then_inc(cols_ready, 1)
            dve.tensor_copy(convw[:, :], pair[1][:, P:P + 3 * H * TAPS]).then_inc(cols_ready, 1)
            dve.wait_ge(consts_done, 1)
            dve.tensor_reduce(lower_row[:, :], level[:, :, :], mybir.AxisListType.X, ALU.max)\
                .then_inc(lower_rows, 1)
            dve.wait_ge(lower_rows, 1)
            dve.tensor_scalar(lower_row[:, :], lower_row[:, :], -1.0, 1.0, ALU.mult, ALU.add).then_inc(lower_rows, 1)
            dve.wait_ge(silu_c, 1)
            for n in range(2 * KT):
                kt, part = n // 2, n % 2
                dve.wait_ge(ada_loaded[n % 6], 16 * (n // 6 + 1))
                if kt == 0:
                    dve.tensor_scalar(acc[:, part, :], ada[:, n % 6, :], c_col[:, kt:kt + 1], None, ALU.mult)\
                        .then_inc(ada_added, 1)
                else:
                    dve.wait_ge(ada_added, n - 1)
                    dve.scalar_tensor_tensor(out=acc[:, part, :], in0=ada[:, n % 6, :], scalar=c_col[:, kt:kt + 1],
                                             in1=acc[:, part, :], op0=ALU.mult, op1=ALU.add).then_inc(ada_added, 1)
                if n % 3 == 1 and n // 3 < NB:
                    scale_x(dve, n // 3)
            dve.wait_ge(mod_summed, 1)
            dve.tensor_tensor(mod[:, :], pair[0][:, 0:2 * KT], b_col[:, 0:2 * KT], ALU.add).then_inc(mod_biased, 1)
            dve.wait_ge(mod_biased, 1)
            dve.tensor_copy(s_col[:, :], mod[:, 0:KT]).then_inc(mod_biased, 1)
            dve.wait_ge(mod_biased, 2)
            dve.scalar_tensor_tensor(out=a_col[:, :], in0=mod[:, KT:2 * KT], scalar=1.0, in1=g_col,
                                     op0=ALU.add, op1=ALU.mult).then_inc(mod_cols, 1)
            dve.wait_ge(gates_zeroed, 3)
            dve.tensor_tensor(gatecol[:, 1:2], gatecol[:, 1:2], gatecol[:, 0:1], ALU.mult).then_inc(gates_dve, 1)
            dve.tensor_scalar(qgain, qgain, SCALE, None, ALU.mult).then_inc(gates_dve, 1)
            for kt in range(KT):
                dve.wait_ge(h_affine, kt + 1)
                dve.tensor_copy(h_hi[:, kt, :], xT[:, kt, :]).then_inc(h_hi_done, 1)
                if kt % 2 == 0:
                    dve.wait_ge(h_hi_done, kt + 1)
                    dve.tensor_tensor(h_lo[:, kt, :], xT[:, kt, :], h_hi[:, kt, :].bitcast(F32), ALU.subtract)\
                        .then_inc(h_lo_even, 1)

            def conv_tap_of(m, n, i):
                used = (D0 + n) % 2
                t = (vT, gq, gk)[n][:, i:SEQ]
                if i == 1:
                    dve.wait_ge(conv_first, 3 * m + n + 1)
                else:
                    dve.wait_ge(conv_tap, 9 * m + 3 * n + i - 1)
                dve.scalar_tensor_tensor(out=t, in0=pair[used][:, 0:SEQ - i],
                                         scalar=hconv[:, CONV_AT[n], TAPS - 1 - i:TAPS - i], in1=t,
                                         op0=ALU.mult, op1=ALU.add).then_inc(conv_tap, 1)

            def conv(m, slot):
                if slot == 0:
                    dve.tensor_copy(hconv[:, :, :], convw[:, :].rearrange("p (k s h) -> p s k h", k=TAPS, s=3)
                                    [:, :, :, bass.ds(m, 1)].rearrange("p s k o -> p s (k o)"))\
                        .then_inc(head_conv, 1)
                for n in range(3):
                    for i in range(1, TAPS):
                        if slot == KT * (n + 1) + i:
                            conv_tap_of(m, n, i)

            r, e, w, ln = fq[0:64, :], fk[0:64, :], fz[0:64, :], flatb(fv)[0:64, :]
            done = [2]

            def step(ins):
                ins.then_inc(gates_dve, 1)
                done[0] += 1
                dve.wait_ge(gates_dve, done[0])

            dve.wait_ge(gates_act, 5)
            step(dve.tensor_scalar(w, e, 1.0, None, ALU.add))
            dve.wait_ge(gates_act, 6)
            step(dve.scalar_tensor_tensor(out=e, in0=w, scalar=-1.0, in1=e, op0=ALU.add, op1=ALU.subtract))
            step(dve.reciprocal(w, w))
            step(dve.scalar_tensor_tensor(out=e, in0=e, scalar=-1.0, in1=w, op0=ALU.mult, op1=ALU.mult))
            step(dve.tensor_tensor(ln, ln, e, ALU.add))
            step(dve.scalar_tensor_tensor(out=r, in0=r, scalar=0.0, in1=ln, op0=ALU.max, op1=ALU.add))
            step(dve.scalar_tensor_tensor(out=gatecol[0:64, 3:4], in0=gatecol[0:64, 2:3], scalar=-1.0,
                                          in1=gatecol[0:64, 0:1], op0=ALU.mult, op1=ALU.mult))
            step(dve.tensor_scalar(r, r, gatecol[0:64, 3:4], None, ALU.mult))
            step(dve.tensor_tensor_scan(fq[0:H, :], ones[0:H, 0:1].to_broadcast([H, SEQ]), fq[0:H, :], 0.0,
                                        ALU.mult, ALU.add))
            for j in range(NB):
                g = blk(fq[32:32 + H, :], j)
                step(dve.tensor_tensor_scan(g, ones[32:32 + H, 0:1].to_broadcast([H, P]), g, 0.0,
                                            ALU.mult, ALU.add))
            step(dve.tensor_scalar(fq[64:96, :], fq[64:96, :], 1.0, None, ALU.add))
            step(dve.reciprocal(fq[64:96, :], fq[64:96, :]))
            assert done[0] == GATES_ROWS
            def gates_turned_out():
                dve.wait_ge(gates_turned, 1)
                for i, row in enumerate((32, 64)):
                    src = blocks(mAB)[:, :, row:row + H].rearrange("p j h -> p h j")
                    dve.tensor_copy(gcol[:, :, i * NB:(i + 1) * NB], src).then_inc(gates_cols, 1)

            conv(0, 0)
            for i in range(1, TAPS):
                conv_tap_of(0, 0, i)
            for kt in range(KT):
                if kt in (6, 12):
                    for i in range(1, TAPS):
                        conv_tap_of(0, kt // 6, i)
                if kt == 12:
                    gates_turned_out()
                dve.wait_ge(gate_loaded[kt % 2], 16 * (kt // 2 + 1))
                if kt == 0:
                    dve.tensor_scalar(acc_gate, ada_gate[0], c_col[:, 0:1], None, ALU.mult).then_inc(gate_added, 1)
                else:
                    dve.wait_ge(gate_added, kt)
                    dve.scalar_tensor_tensor(out=acc_gate, in0=ada_gate[kt % 2], scalar=c_col[:, kt:kt + 1],
                                             in1=acc_gate, op0=ALU.mult, op1=ALU.add).then_inc(gate_added, 1)
            dve.wait_ge(gate_summed, 1)
            dve.wait_ge(gate_biased, 16)
            dve.tensor_tensor(ada_gate[1][0:1, :], flat(ps[0:1, 4:8, :]), ada_gate[0][0:1, :], ALU.add)\
                .then_inc(gate_row, 1)
            dve.wait_ge(gates_cols, 2)

            def fox(m, slot, gap=GAP):
                for i, (at, t, gain) in enumerate(((4, fq, qgain), (5, fk, kgain))):
                    if slot == at:
                        dve.wait_ge(fox_rstd, 2 * m + i + 1)
                        dve.scalar_tensor_tensor(out=t[:, :], in0=t[:, :], scalar=gain, in1=f_s[i],
                                                 op0=ALU.mult, op1=ALU.mult).then_inc(fox_qk, 1)
                if slot == 6:
                    for g in range(2):
                        dve.wait_ge(fox_vturn, 2 * m + g + 1)
                        dve.tensor_copy(fv[:, 4 * g:4 * g + 4, :], blocks((mC, mD)[g], 4)).then_inc(fox_v, 1)
                for n in range(NB):
                    i = NB - 1 - n
                    at = fox_slot(n, gap)
                    L = (i + 1) * P
                    s = f_s[n % 2][:, 0:L]
                    if slot == at + 1:
                        dve.wait_ge(fox_scores, 8 * m + n + 1)
                        dve.wait_ge(fox_masked, 8 * m + n + 1)
                        if n >= 2:
                            dve.wait_ge(fox_pturn, GROUPS * m + groups_before(n - 1))
                        dve.memset(dummy[:, :], 0.0)
                        dve.tensor_tensor_reduce(s, mAB[:, 0:L], f_bias[:, 0:L], -1.0, BIG, ALU.add, ALU.min,
                                                 negmax[:, n:n + 1]).then_inc(fox_max, 1)
                    if slot == at + 3:
                        dve.wait_ge(fox_exp, 8 * m + n + 1)
                        dve.reciprocal(rsum[:, n:n + 1], lsum[:, n:n + 1]).then_inc(fox_recip, 1)
                        dve.wait_ge(fox_recip, 8 * m + n + 1)
                        dve.tensor_scalar(s, s, rsum[:, n:n + 1], None, ALU.mult).then_inc(fox_probs, 1)
                    for g in range(n_groups(n)):
                        if slot == at + 4 + g:
                            k = min(4, i + 1 - 4 * g)
                            dve.wait_ge(fox_pturn, GROUPS * m + groups_before(n) + g + 1)
                            if n and g == 0:
                                dve.wait_ge(fox_pv, 8 * m + n)
                            dve.tensor_copy(f_pt[:, 4 * g:4 * g + k, :], blocks(mC, 4)[:, 0:k, :]).then_inc(fox_pt, 1)
                    if slot == at + 6 and n in (3, 7):
                        hv = half(fz[:, :], 1 if n == 3 else 0)
                        dve.wait_ge(fox_pv, 8 * m + n + 1)
                        dve.tensor_tensor(hv, mD, hv, ALU.mult).then_inc(fox_half, 1)

            def gdn(m, slot):
                if slot == 0:
                    dve.tensor_copy(hcol[:, :], gcol[:, bass.ds(m, 1), :].rearrange("p o k -> p (o k)"))\
                        .then_inc(gdn_cols, 1)
                    dve.wait_ge(gdn_cols, 4 * m + 1)
                    dve.wait_ge(dec_in, 16 * m + 16)
                    last = g_dec.rearrange("p (b q) -> p q b", q=P)[:, P - 1, :]
                    dve.tensor_tensor(edl[:, :], last, hcol[:, 0:NB], ALU.subtract).then_inc(gdn_cols, 1)
                    dve.tensor_scalar(negbeta[:, :], hcol[:, NB:], -1.0, None, ALU.mult).then_inc(gdn_cols, 1)
                    for j in range(NB):
                        dve.scalar_tensor_tensor(out=blk(g_t, j), in0=blk(g_dec, j), scalar=hcol[:, j:j + 1],
                                                 in1=strict[:, :], op0=ALU.subtract, op1=ALU.add)\
                            .then_inc(gdn_args, 1)
                if slot == 3:
                    for j in range(NB):
                        dve.scalar_tensor_tensor(out=blk(g_att, j), in0=blk(g_dec, j), scalar=hcol[:, j:j + 1],
                                                 in1=causal_t[:, :], op0=ALU.subtract, op1=ALU.add)\
                            .then_inc(gdn_args, 1)
                if slot in (4, 5):
                    i = slot - 4
                    t, rs = ((gq, view(1)), (gk, view(3)))[i]
                    dve.wait_ge(gdn_rstd, 2 * m + i + 1)
                    dve.scalar_tensor_tensor(out=t[:, :], in0=t[:, :], scalar=(SCALE, 1.0)[i], in1=rs,
                                             op0=ALU.mult, op1=ALU.mult).then_inc(gdn_qk, 1)
                if slot == 6:
                    dve.wait_ge(gdn_cexp, 2 * m + 2)
                    dve.wait_ge(gdn_cols, 4 * m + 3)
                    dve.tensor_tensor(negbg[:, :], eg[:, :], negbeta[:, :], ALU.mult).then_inc(gdn_cols, 1)
                if slot == 7:
                    for g in range(2):
                        dve.wait_ge(gdn_vturn, 2 * m + g + 1)
                        dve.tensor_tensor(gv[:, 4 * g:4 * g + 4, :], blocks((mA, mB)[g], 4),
                                          spread(hcol[:, NB + 4 * g:NB + 4 * g + 4], 4), ALU.mult).then_inc(gdn_v, 1)
                if slot == 8:
                    for g in range(2):
                        dve.wait_ge(gdn_kturn, 2 * m + g + 1)
                        dve.tensor_tensor(blocks(half(g_kdec, g), 4), blocks((mC, mD)[g], 4),
                                          spread(edl[:, 4 * g:4 * g + 4], 4), ALU.mult).then_inc(gdn_kdec, 1)
                if slot == 10:
                    dve.wait_ge(gdn_decays, 3 * m + 1)
                    for j in range(NB):
                        dve.wait_ge(gdn_gram, 2 * m + j // 4 + 1)
                        dve.scalar_tensor_tensor(out=blk(g_n, j), in0=blk(mAB, j), scalar=negbeta[:, j:j + 1],
                                                 in1=blk(g_t, j), op0=ALU.mult, op1=ALU.mult).then_inc(gdn_n, 1)
                if slot == 11:
                    dve.wait_ge(gdn_decays, 3 * m + 2)
                    for g in range(2):
                        dve.wait_ge(gdn_att_mm, 2 * m + g + 1)
                        dve.tensor_tensor(half(g_att, g), (mC, mD)[g], half(g_att, g), ALU.mult).then_inc(gdn_att, 1)
                if slot == 12:
                    for g in range(2):
                        dve.wait_ge(gdn_n, 8 * m + 4 * g + 4)
                        dve.tensor_tensor(blocks(half(g_t, g), 4), blocks(half(g_n, g), 4),
                                          over_blocks(level[:, 0, :], 4), ALU.mult).then_inc(gdn_t0, 1)
                    for g in range(2):
                        dve.wait_ge(gdn_t0, 2 * m + g + 1)
                        dve.tensor_tensor(blocks(half(g_t, g), 4), blocks(half(g_t, g), 4),
                                          over_blocks(ident[:, :], 4), ALU.add).then_inc(gdn_t1, 1)
                L = LEVELS - 1
                for lv in range(1, LEVELS):
                    i = lv - 1
                    if slot == INV0 + 2 * i:
                        for g in range(2):
                            dve.wait_ge(inv_p, 2 * L * m + 2 * i + g + 1)
                            keep_it = side(level[:, lv, :], lv, 0)
                            dve.tensor_tensor(sides(half(g_n, g), lv, 0), compact((mA, mB)[g], lv),
                                              keep_it.unsqueeze(1).to_broadcast([P, 4] + list(keep_it.shape[1:])),
                                              ALU.mult).then_inc(inv_p_out, 1)
                    if slot == INV0 + 2 * i + 1:
                        for g in range(2):
                            if lv < LEVELS - 1:
                                dve.wait_ge(inv_t, 2 * (L - 1) * m + 2 * i + g + 1)
                                t = sides(half(g_t, g), lv, 0)
                                dve.tensor_tensor(t, compact((mC, mD)[g], lv), t, ALU.add)\
                                    .then_inc(inv_t_out, 1)
                            dve.wait_ge(inv_u, 2 * L * m + 2 * i + g + 1)
                            u = sides(half(g_u, g), lv, 1)
                            dve.scalar_tensor_tensor(out=u, in0=compact((mA, mB)[g], lv),
                                                     scalar=lower_row[:, lv:lv + 1], in1=u,
                                                     op0=ALU.mult, op1=ALU.add)\
                                .then_inc(inv_u_out, 1)
                for j in range(NB):
                    at = scan_slot(j)
                    if slot == at and j > 0:
                        dve.wait_ge(scan_z, 7 * m + j)
                        dve.scalar_tensor_tensor(out=ybuf[j % 2], in0=mA[:, 0:P], scalar=negbg[:, j:j + 1],
                                                 in1=gv[:, j, :], op0=ALU.mult, op1=ALU.add).then_inc(scan_y, 1)
                    if slot == at + 2 and j < NB - 1:
                        dve.wait_ge(scan_upd, 7 * m + j + 1)
                        if j == 0:
                            dve.tensor_copy(state[1], mC[:, 0:P]).then_inc(scan_state, 1)
                        else:
                            dve.wait_ge(scan_state, 7 * m + j)
                            dve.scalar_tensor_tensor(out=state[(j + 1) % 2], in0=state[j % 2],
                                                     scalar=g_dec[:, j * P + P - 1:j * P + P], in1=mC[:, 0:P],
                                                     op0=ALU.mult, op1=ALU.add).then_inc(scan_state, 1)
                if slot == SLOTS - 3:
                    dve.wait_ge(out_rstd, m + 1)
                    dve.scalar_tensor_tensor(out=g_o, in0=g_o, scalar=ngain, in1=g_t,
                                             op0=ALU.mult, op1=ALU.mult).then_inc(out_norm, 1)
                    dve.wait_ge(gdn_z, m + 1)
                    dve.wait_ge(out_norm, m + 1)
                    dve.tensor_tensor(g_o, g_o, gz[:, :], ALU.mult).then_inc(gdn_done, 1)

            def part_B(m):
                for slot in range(SLOTS):
                    fox(m, slot)
                    conv(m + 1, slot)

            def part_A(m):
                for slot in range(SLOTS):
                    gdn(m, slot)

            part_A(0)
            part_B(0)
            with dve.Fori(1, H - 1) as m:
                part_A(m)
                part_B(m)
            part_A(H - 1)

            def split_m(n, i, src, cols=slice(0, SEQ)):
                dve.wait_ge(m_hi_done, n + 1)
                dve.tensor_tensor(m_lo[:, i, cols], src, m_hi[:, i, cols].bitcast(F32), ALU.subtract)\
                    .then_inc(m_lo_done, 1)

            split_m(0, ORDER[0], g_o)
            for slot in range(LAST_SLOTS):
                fox(H - 1, slot, LAST_GAP)
                k = (slot - 2) // 2
                if slot % 2 == 0 and 0 < k < KT - 1:
                    split_m(k, ORDER[k], staged[k % 4])
                elif slot % 2 == 0 and k == KT - 1:
                    split_m(k, H - 1, half(fz[:, :], 1), slice(HALF, SEQ))
            split_m(KT, H - 1, half(fz[:, :], 0), slice(0, HALF))

            dve.wait_ge(gate_in, 16)
            for idx in range(8):
                hf, ch = idx // 4, idx % 4
                for t in range(4):
                    dve.wait_ge(y_ready, 4 * idx + t + 1)
                    if idx:
                        dve.wait_ge(y_added, 4 * (idx - 1) + t + 1)
                    dve.tensor_tensor(gated[:, t, :], ps[:, idx % 2 * 4 + t, :],
                                      gate_all[:, ch * HALF:(ch + 1) * HALF], ALU.mult).then_inc(y_gated, 1)
                if ch == 3:
                    if hf == 0:
                        dve.wait_ge(final_g_in, 16)
                    for t in range(4):
                        k = 4 * hf + t
                        dve.wait_ge(y_sq, 4 * idx + t + 1)
                        dve.tensor_reduce(xstat[:, 16 + t:17 + t], xstat[:, 4 * t:4 * t + 4],
                                          mybir.AxisListType.X, ALU.add).then_inc(y_sum, 1)
                        dve.wait_ge(y_rstd, k + 1)
                        dve.scalar_tensor_tensor(out=y[:, t, :], in0=y[:, t, :], scalar=xstat[:, 24 + t:25 + t],
                                                 in1=fg_all[:, :], op0=ALU.mult, op1=ALU.mult).then_inc(y_done, 1)


_INS = ['x', 'c', 'norm_g', 'w_ada', 'b_ada', 'w_in', 'b_fgate', 'fox_qn_g', 'fox_kn_g',
        'gdn_conv_w', 'gdn_A_log', 'gdn_dt_bias', 'gdn_norm_g', 'w_out', 'final_g']


def kernel(**inputs):
    import numpy as _np
    import concourse.bacc as _bacc
    from concourse import mybir as _mybir
    from concourse.bass_utils import run_bass_kernel_spmd as _run

    nc = _bacc.Bacc("TRN2", target_bir_lowering=False, num_devices=1, dynamic_dma_scratch_size=1024)
    arrays, args = {}, []
    for name in _INS:
        a = _np.ascontiguousarray(inputs[name])
        arrays[f"in_{name}_dram"] = a
        args.append(nc.dram_tensor(f"in_{name}_dram", a.shape, _mybir.dt.from_np(a.dtype), kind="ExternalInput").ap())
    shape = inputs['x'].shape
    args.append(nc.dram_tensor("out_0_dram", shape, _mybir.dt.float32, kind="ExternalOutput").ap())
    hybrid_block(nc, *args)
    r = _run(nc, [arrays], core_ids=[0])
    return r.results[0]["out_0_dram"]
```
